# Optimizing a Trainium2 kernel written in Bass

```python
import jax, jax.numpy as jnp
from jax import lax
import numpy as np

D_MODEL = 1024
BATCH = 1
SEQ = 256
DEPTH = 1
DEC_BATCH = 8
DEC_SEQ = 8
PAST_LEN = 2048
PAGE_SIZE = 128

D_CONV = D_MODEL // 2
CONV_WIDTH = 3
D_POOL = D_MODEL // 2
POOL_WINDOWS = (2, 4, 8, 16)
N_POOL_GROUPS = len(POOL_WINDOWS)
POOL_GROUP = D_POOL // N_POOL_GROUPS
POOL_HIST = max(POOL_WINDOWS) - 1
D_IN_PROJ = 3 * D_CONV + D_POOL + 2 * D_MODEL
SPLITS = [D_CONV, 2 * D_CONV, 3 * D_CONV, 3 * D_CONV + D_POOL, 3 * D_CONV + D_POOL + D_MODEL]
N_EXPERTS = 32
TOP_K = 4
D_EXPERT = D_MODEL
SWIGLU_LIMIT = 7.0
SWIGLU_ALPHA = 1.702
MOE_BLOCK = 128
LN_EPS = 1e-5
DEEPNORM_ALPHA = (2 * DEPTH) ** 0.25
DEEPNORM_BETA = (8 * DEPTH) ** -0.25

kernel_name = "hybrid_conv_pool_moe_decode_step"

def layer_norm(x, g, b):
    xf = x.astype(jnp.float32)
    mu = jnp.mean(xf, axis=-1, keepdims=True)
    xc = xf - mu
    var = jnp.mean(xc * xc, axis=-1, keepdims=True)
    y = xc * lax.rsqrt(var + LN_EPS) * g.astype(jnp.float32) + b.astype(jnp.float32)
    return y.astype(x.dtype)

def multiscale_pool(pc, T, start):
    s = jnp.cumsum(pc.astype(jnp.float32), axis=1)
    s = jnp.pad(s, ((0, 0), (1, 0), (0, 0)))
    H = POOL_HIST
    pos = start + jnp.arange(T)
    outs = []
    for g, w in enumerate(POOL_WINDOWS):
        sl = slice(g * POOL_GROUP, (g + 1) * POOL_GROUP)
        win = s[:, H + 1:H + 1 + T, sl] - s[:, H + 1 - w:H + 1 - w + T, sl]
        cnt = jnp.minimum(w, pos + 1).astype(jnp.float32)[None, :, None]
        outs.append(win / cnt - pc[:, H:, sl].astype(jnp.float32))
    return jnp.concatenate(outs, axis=-1).astype(pc.dtype)

def moe_ffn(xf, w_router, b_router, w_up, b_up, w_down, b_down):
    T, D = xf.shape
    logits = (xf @ w_router + b_router).astype(jnp.float32)
    top_vals, top_idx = lax.top_k(logits, TOP_K)
    gates = jax.nn.softmax(top_vals, axis=-1)
    tk = T * TOP_K
    flat_e = top_idx.reshape(-1)
    order = jnp.argsort(flat_e)
    sorted_e = flat_e[order]
    sorted_tok = order // TOP_K
    counts = jnp.bincount(flat_e, length=N_EXPERTS)
    group_start = jnp.cumsum(counts) - counts
    padded = (counts + MOE_BLOCK - 1) // MOE_BLOCK * MOE_BLOCK
    pad_end = jnp.cumsum(padded)
    pad_start = pad_end - padded
    dest = pad_start[sorted_e] + jnp.arange(tk) - group_start[sorted_e]
    n_blocks = -(-tk // MOE_BLOCK) + N_EXPERTS
    block_e = jnp.minimum(
        jnp.searchsorted(pad_end, jnp.arange(n_blocks) * MOE_BLOCK, side='right'), N_EXPERTS - 1)
    x_pad = jnp.zeros((n_blocks * MOE_BLOCK, D), xf.dtype).at[dest].set(xf[sorted_tok])

    def expert_block(args):
        xb, e = args
        h = xb @ w_up[e] + b_up[e]
        glu = jnp.minimum(h[:, :D_EXPERT], SWIGLU_LIMIT)
        lin = jnp.clip(h[:, D_EXPERT:], -SWIGLU_LIMIT, SWIGLU_LIMIT)
        act = glu * jax.nn.sigmoid(SWIGLU_ALPHA * glu) * (lin + 1)
        return act @ w_down[e] + b_down[e]

    y_pad = lax.map(expert_block, (x_pad.reshape(n_blocks, MOE_BLOCK, D), block_e))
    y_pad = y_pad.reshape(n_blocks * MOE_BLOCK, D)
    contrib = y_pad[dest].astype(jnp.float32) * gates.reshape(-1)[order][:, None]
    return jnp.zeros((T, D), jnp.float32).at[sorted_tok].add(contrib).astype(xf.dtype)

def decoder_layer(x, c, conv_hist, pool_hist, start, w_ada, b_ada, w_in, conv_w, w_out_a,
                  w_pool, ls_pool, w_out_b, w_o, ln1_g, ln1_b, w_router, b_router,
                  w_up, b_up, w_down, b_down, ln2_g, ln2_b):
    Bn, T, D = x.shape
    mod = jax.nn.silu(c) @ w_ada + b_ada
    shift1, scale1, gate1, shift2, scale2, gate2 = jnp.split(mod[:, None, :], 6, axis=-1)

    u = x * (1 + scale1) + shift1
    proj = u @ w_in
    b_g, c_g, xa, xp, g_a, g_b = jnp.split(proj, SPLITS, axis=-1)

    z = c_g * xa
    zc = jnp.concatenate([conv_hist.astype(z.dtype), z], axis=1)
    conv = conv_w[0] * zc[:, :T] + conv_w[1] * zc[:, 1:T + 1] + conv_w[2] * zc[:, 2:T + 2]
    y_a = (b_g * conv) @ w_out_a

    pc = jnp.concatenate([pool_hist.astype(xp.dtype), xp], axis=1)
    diff = multiscale_pool(pc, T, start)
    yg = jnp.einsum('btgc,gcd->btgd', diff.reshape(Bn, T, N_POOL_GROUPS, POOL_GROUP), w_pool)
    y_b = (yg.reshape(Bn, T, D_POOL) * ls_pool) @ w_out_b

    merged = jax.nn.sigmoid(g_a) * y_a + jax.nn.sigmoid(g_b) * y_b
    h = layer_norm(DEEPNORM_ALPHA * x + gate1 * (merged @ w_o), ln1_g, ln1_b)

    v = h * (1 + scale2) + shift2
    f = moe_ffn(v.reshape(Bn * T, D), w_router, b_router, w_up, b_up, w_down, b_down)
    y = layer_norm(DEEPNORM_ALPHA * h + gate2 * f.reshape(Bn, T, D), ln2_g, ln2_b)
    return y, zc[:, -(CONV_WIDTH - 1):], pc[:, -POOL_HIST:]

def setup_inputs(seed: int = 0) -> dict:
    key = jax.random.key(seed)
    ks = jax.random.split(key, 26)

    def nrm(k, shape, scale):
        return jax.random.normal(k, shape, jnp.float32) * scale

    L, D, E, F = DEPTH, D_MODEL, N_EXPERTS, D_EXPERT
    return {
        "x_prompt": nrm(ks[0], (BATCH, SEQ, D), 1.0),
        "x_sample": nrm(ks[1], (DEC_BATCH, DEC_SEQ, D), 1.0),
        "c_prompt": nrm(ks[2], (BATCH, D), 1.0),
        "c_sample": nrm(ks[3], (DEC_BATCH, D), 1.0),
        "state_conv": nrm(ks[4], (L, DEC_BATCH, CONV_WIDTH - 1, D_CONV), 1.0),
        "state_pool": nrm(ks[5], (L, DEC_BATCH, POOL_HIST, D_POOL), 1.0),
        "w_ada": nrm(ks[6], (L, D, 6 * D), 0.5 * D ** -0.5),
        "b_ada": nrm(ks[7], (L, 6 * D), 0.02),
        "w_in": nrm(ks[8], (L, D, D_IN_PROJ), D ** -0.5),
        "conv_w": nrm(ks[9], (L, CONV_WIDTH, D_CONV), CONV_WIDTH ** -0.5),
        "w_out_a": nrm(ks[10], (L, D_CONV, D), D_CONV ** -0.5),
        "w_pool": nrm(ks[11], (L, N_POOL_GROUPS, POOL_GROUP, POOL_GROUP), POOL_GROUP ** -0.5),
        "ls_pool": 1.0 + nrm(ks[12], (L, D_POOL), 0.02),
        "w_out_b": nrm(ks[13], (L, D_POOL, D), D_POOL ** -0.5),
        "w_o": nrm(ks[14], (L, D, D), DEEPNORM_BETA * D ** -0.5),
        "ln1_g": 1.0 + nrm(ks[15], (L, D), 0.02),
        "ln1_b": nrm(ks[16], (L, D), 0.02),
        "w_router": nrm(ks[17], (L, D, E), D ** -0.5),
        "b_router": nrm(ks[18], (L, E), 0.01),
        "w_up": nrm(ks[19], (L, E, D, 2 * F), D ** -0.5),
        "b_up": nrm(ks[20], (L, E, 2 * F), 0.02),
        "w_down": nrm(ks[21], (L, E, F, D), DEEPNORM_BETA * F ** -0.5),
        "b_down": nrm(ks[22], (L, E, D), 0.02),
        "ln2_g": 1.0 + nrm(ks[23], (L, D), 0.02),
        "ln2_b": nrm(ks[24], (L, D), 0.02),
    }

def reference(x_prompt, x_sample, c_prompt, c_sample, state_conv, state_pool, w_ada, b_ada,
              w_in, conv_w, w_out_a, w_pool, ls_pool, w_out_b, w_o, ln1_g, ln1_b,
              w_router, b_router, w_up, b_up, w_down, b_down, ln2_g, ln2_b):
    yp, ys = x_prompt, x_sample
    conv_p, pool_p, conv_s, pool_s = [], [], [], []
    for l in range(DEPTH):
        lw = (w_ada[l], b_ada[l], w_in[l], conv_w[l], w_out_a[l], w_pool[l], ls_pool[l],
              w_out_b[l], w_o[l], ln1_g[l], ln1_b[l], w_router[l], b_router[l],
              w_up[l], b_up[l], w_down[l], b_down[l], ln2_g[l], ln2_b[l])
        zero_conv = jnp.zeros((yp.shape[0], CONV_WIDTH - 1, D_CONV), yp.dtype)
        zero_pool = jnp.zeros((yp.shape[0], POOL_HIST, D_POOL), yp.dtype)
        yp, cp, pp = decoder_layer(yp, c_prompt, zero_conv, zero_pool, 0, *lw)
        ys, cs, ps = decoder_layer(ys, c_sample, state_conv[l], state_pool[l], PAST_LEN, *lw)
        conv_p.append(cp)
        pool_p.append(pp)
        conv_s.append(cs)
        pool_s.append(ps)
    return (yp, ys, jnp.stack(conv_p), jnp.stack(pool_p), jnp.stack(conv_s), jnp.stack(pool_s))


_drawn_inputs = setup_inputs


def setup_inputs(seed=0):
    import zlib

    import numpy as np

    out = dict(_drawn_inputs(seed))
    spreads = {}
    factors = {'ls_pool': 33.834,
     'b_router': 26.016,
     'b_up': 26.596,
     'b_down': 42.538,
     'ln2_g': 24.454,
     'ln2_b': 23.958,
     'ln1_g': 2.679,
     'state_conv': 4.571,
     'ln1_b': 5.989}
    for name, (base, spread) in spreads.items():
        noise = np.random.default_rng([zlib.crc32(name.encode()), seed]).standard_normal(out[name].shape)
        drawn = base * np.exp(spread * noise) if base else spread * noise
        out[name] = __import__('jax').numpy.asarray(drawn.astype(out[name].dtype))
    for name, factor in factors.items():
        out[name] = (out[name] * factor).astype(out[name].dtype)
    return out
```

```python
from contextlib import ExitStack

import numpy as np

import concourse.bass as bass
from concourse import mybir

F32 = mybir.dt.float32
BF16 = mybir.dt.bfloat16
I32 = mybir.dt.int32
U32 = mybir.dt.uint32
ALU = mybir.AluOpType
ACT = mybir.ActivationFunctionType
AX_X = mybir.AxisListType.X

P = 128
D = 1024
DC = 512
KC = D // P
NP_TOK = 256
NSEQ, TSEQ = 8, 8
NS_TOK = NSEQ * TSEQ
NT = NP_TOK + NS_TOK
ROWS = (P, P, NS_TOK)
NC_ROWS = 1 + NSEQ
HIST_C, HIST_P = 2, 15
WINDOWS = (2, 4, 8, 16)
E = 32
TOPK = 4
SLOTS = 64
MAXR = -(-NT // SLOTS)
NROUND = 64
LIMIT, SWISH = 7.0, 1.702
EPS = 1e-5
ALPHA = 2.0 ** 0.25

C_ID, C_TRI, C_ONE, C_TRI1, C_IOTA, C_INV = 0, 128, 256, 384, 416, 736
C_SEL = C_INV + 4 * HIST_P
C_N = C_SEL + E

RING = 6
CH = 4096
EXPERT_CHUNKS = 6
FRONT_CHUNKS = 24

FRONT = (
    ["c_T", "chan_T"] + ["ada0", "mod_T"] + [f"x_T{k}" for k in range(KC)] + ["conv_hist_T", "pool_hist_T"]
    + [f"proj{m}" for m in (4, 5, 6, 7, 8, 9, 10, 11, 0, 1, 2, 3, 12, 13, 14, 15)]
    + [f"proj{m}" for m in range(16, 32)]
    + [f"pool{g}" for g in range(4)]
    + ["state_cp", "state_cs", "state_pp", "state_ps"] + ["ada1", "ada2"]
    + [f"out_a{m}" for m in range(8)] + [f"out_b{m}" for m in range(8)]
    + [f"o{t}{h}" for t in range(3) for h in range(2)]
    + [f"v_T{k}" for k in range(KC)] + ["logits", "rank", "counts", "bounds", "table", "gate_T"]
)
B_UP, B_X, B_DOWN, B_T, B_XT, B_C = (0, 1), 2, 3, 4, 5, (6, 7)
COMBINE_BANKS = (6, 7, 6, 7, 6)
PER_ROUND = [1, 1, 1, 1, 2, 1, 3, 2]


def front_place(name):
    n = FRONT.index(name)
    return n % 8, n // 8


def front_uses(bank):
    return len([n for n in range(len(FRONT)) if n % 8 == bank])


def program(nc, a, o):
    ctx = ExitStack()
    with ctx:
        def sb(name, shape, dt=F32):
            return ctx.enter_context(nc.sbuf_tensor(name, shape, dt))

        def sem(name):
            return ctx.enter_context(nc.semaphore(name))

        ring = sb("ring", [P, RING, CH])
        front = sb("front", [P, 18720])
        hx = sb("hx", [P, 3, D])
        tail_rows = sb("tail_rows", [P, 4 * D])
        const = sb("const", [P, C_N])
        small = sb("small", [P, 700])
        table = sb("table", [1, 192], I32)
        top_index = sb("top_index", [P, 3, 8], U32)
        mod_rows = nc.dram_tensor("mod_rows", [NC_ROWS, 6 * D], F32)
        bank = [ctx.enter_context(nc.psum_tensor(f"bank{b}", [P, 512], F32)) for b in range(8)]

        def region(t, at, *shape):
            n = int(np.prod(shape))
            v = t[:, at:at + n]
            if len(shape) == 2:
                return v.rearrange("p (a b) -> p a b", a=shape[0])
            if len(shape) == 3:
                return v.rearrange("p (a b c) -> p a b c", a=shape[0], b=shape[1])
            return v

        ident = const[:, C_ID:C_ID + P]
        tri = const[:, C_TRI:C_TRI + P]
        ones = const[:, C_ONE:C_ONE + P]
        tri_incl = const[:, C_TRI1:C_TRI1 + E]
        iota = const[:, C_IOTA:C_IOTA + NT]
        sel3 = const[:, C_SEL:C_SEL + E]
        inv_count = region(const, C_INV, 4, HIST_P)

        u_T = region(front, 0, KC, NT)
        b_T = region(front, 2560, 4, NT)
        c_T = region(front, 3840, 4, NT)
        z_p = region(front, 5120, 4, HIST_C + NP_TOK)
        z_s = region(front, 6152, 4, NSEQ, HIST_C + TSEQ)
        pool_p = region(front, 6472, 4, HIST_P + NP_TOK)
        pool_s = region(front, 7556, 4, NSEQ, HIST_P + TSEQ)
        diff_T = region(front, 8292, 4, NT)
        y_in_T = region(front, 9572, 4, NT)
        yg_T = region(front, 10852, 4, NT)
        ga_T = region(front, 12132, KC, NT)
        gb_T = region(front, 14692, KC, NT)
        sum_p = region(front, 17252, 2, HIST_P + NP_TOK)
        sum_s = region(front, 17800, 2, NSEQ, HIST_P + TSEQ)
        keep_s = region(front, 18168, 4, NSEQ, HIST_C)
        keep_ps = region(front, 18232, 4, NSEQ, HIST_P)
        c_rows = region(front, 12132, D)
        chan_rows = region(front, 13156, P)
        conv_hist = region(front, 10852, DC)
        pool_hist = region(front, 11364, DC)
        mod = region(tail_rows, 0, 3, 512)
        b_ada_rows = region(tail_rows, 1536, 3, 512)
        sg_c = region(small, 0, KC, NC_ROWS)
        sc_T = region(small, 72, KC, NC_ROWS)
        chan = region(small, 144, 16)
        state_rows = region(front, 0, 4, DC)
        V = region(front, 0, 3, D)
        b_up_rows = region(front, 3072, 2 * D)
        b_up_parts = region(front, 5120, D).bitcast(BF16)
        v_T = region(front, 8292, KC, NT)
        S = region(front, 6472, 3, SLOTS)
        S_gate = region(front, 6664, 3, P)
        x_rows = region(front, 7048, 512)
        up_sel = region(front, 7560, SLOTS // 2).bitcast(BF16)
        glu = region(front, 8292, 2, 256)
        lin = region(front, 8804, 2, 256)
        sig = region(front, 9316, 2, 256)
        act_rows = region(front, 9828, 512)
        act_T = region(front, 10340, 4, P)
        x_T = region(front, 10852, 4, P)
        P_gate = region(front, 11364, NT)
        O_rows = region(front, 11684, 2, 512)
        Y = region(front, 14692, 5, 512)
        y2_rows = region(front, 12708, 512)
        w_pool = region(small, 160, 4, P)
        w_router = region(small, 160, KC, E)
        b_router = region(small, 672 - 256, E)
        mod_T = region(front, 17252 - 0, 4, P)
        stats = region(front, 17252, 12)
        aggr = region(front, 17264, 2)
        rstd = region(front, 17266, 1)
        ln_rows = region(front, 10852, D)
        rstd2 = region(front, 17267, 1)
        L = region(front, 17272, 3, E)
        top = region(front, 17368, 3, 8)
        top_f = region(front, 17392, 3, 8)
        mask = region(front, 17416, 3, E)
        eq = region(front, 17512, 3, E)
        gate = region(front, 17608, 3, E)
        gsum = region(front, 17704, 3)
        rank = region(front, 17707, 3, E)
        count = region(front, 17803, 1)
        rounds = region(front, 17804, 1)
        bound = region(front, 17805, 1)
        passed = region(front, 17806, NROUND)
        base_f = region(front, 17870, NROUND)

        bank_full = [sem(f"bank_full{b}") for b in range(8)]
        bank_free = [sem(f"bank_free{b}") for b in range(8)]
        chunk_landed = [sem(f"chunk_landed{s}") for s in range(RING)]
        chunk_used = [sem(f"chunk_used{s}") for s in range(RING)]
        const_landed = sem("const_landed")
        rows_landed = sem("rows_landed")
        x_landed = sem("x_landed")
        hist_landed = sem("hist_landed")
        bada_landed = sem("bada_landed")
        pool_w_landed = sem("pool_w_landed")
        router_landed = sem("router_landed")
        norm1_landed = sem("norm1_landed")
        tail_landed = sem("tail_landed")
        bias_landed = sem("bias_landed")
        mod_stored = sem("mod_stored")
        out_stored = sem("out_stored")
        dve_step = sem("dve_step")
        tail_step = sem("tail_step")
        c_sig_ready = sem("c_sig_ready")
        diff_ready = sem("diff_ready")
        conv_ready = sem("conv_ready")
        v_ready = sem("v_ready")
        keep_ready = sem("keep_ready")
        logit_ready = sem("logit_ready")
        var_ready = sem("var_ready")
        sqrt_ready = sem("sqrt_ready")
        exp_ready = sem("exp_ready")
        mask_ready = sem("mask_ready")
        rounds_ready = sem("rounds_ready")
        passed_ready = sem("passed_ready")
        table_ready = sem("table_ready")
        parts_step = sem("parts_step")
        b_up_ready = sem("b_up_ready")
        b_down_landed = sem("b_down_landed")
        O_cleared = sem("O_cleared")
        softmax_ready = sem("softmax_ready")
        sel_ready = sem("sel_ready")
        S_ready = sem("S_ready")
        gate_ready = sem("gate_ready")
        x_rows_ready = sem("x_rows_ready")
        xT_ready = sem("xT_ready")
        glu_ready = sem("glu_ready")
        sig_ready = sem("sig_ready")
        act_ready = sem("act_ready")
        actT_ready = sem("actT_ready")
        Pg_ready = sem("Pg_ready")
        O_ready = sem("O_ready")
        y_ready = sem("y_ready")

        block = ctx.enter_context(nc.Block())

        def front_slot(n):
            return n % RING

        def expert_slot(c):
            return (c + 2) % RING

        def landed_before(s):
            return len([n for n in range(FRONT_CHUNKS) if n % RING == s])

        def last_result(n):
            if n in (3, 15, 19):
                return f"ada{(3, 15, 19).index(n)}"
            if 4 <= n < 12:
                return f"proj{4 * IN_ORDER[n - 4] + 3}"
            return {20: "out_a7", 21: "out_b7", 23: "o21"}.get(n)

        def used_before(s):
            return len([n for n in range(FRONT_CHUNKS) if n % RING == s and last_result(n) is None])

        def wait_chunk_read(eng, n):
            if last_result(n) is None:
                s = n % RING
                eng.wait_ge(chunk_used[s], len([m for m in range(n + 1) if m % RING == s and last_result(m) is None]))
            else:
                wait_full(eng, last_result(n))

        IN_ORDER = (1, 2, 0, 3, 4, 5, 6, 7)
        ADA_CHUNK = [0, 12, 16]
        IN_CHUNK, OUTA_CHUNK, OUTB_CHUNK, O_CHUNK = 4, 20, 21, 22

        def wait_full(eng, name):
            b, n = front_place(name)
            eng.wait_ge(bank_full[b], n + 1)
            return bank[b]

        def wait_read(eng, name):
            b, n = front_place(name)
            eng.wait_ge(bank_free[b], n + 1)

        @block.sync
        def _(sp):
            w_ada = a["w_ada"][0].rearrange("(k p) n -> p k n", p=P)
            w_in = a["w_in"][0].rearrange("(k p) n -> p k n", p=P)

            def front_chunk(n, src, shape):
                s = front_slot(n)
                if n >= RING:
                    wait_chunk_read(sp, n - RING)
                dst = ring[:, s, :].rearrange("p (a b) -> p a b", a=shape[0])
                sp.dma_start(dst, src).then_inc(chunk_landed[s], 16)

            for i in range(4):
                front_chunk(ADA_CHUNK[0] + i, w_ada[:, 2 * i:2 * i + 2, 0:2048], (2, 2048))
            for i in range(8):
                m = IN_ORDER[i]
                front_chunk(IN_CHUNK + i, w_in[:, :, m * 512:(m + 1) * 512], (8, 512))
            for third in (1, 2):
                for i in range(4):
                    front_chunk(ADA_CHUNK[third] + i,
                                w_ada[:, 2 * i:2 * i + 2, third * 2048:(third + 1) * 2048], (2, 2048))
            front_chunk(OUTA_CHUNK, a["w_out_a"][0].rearrange("(k p) n -> p k n", p=P), (4, D))
            front_chunk(OUTB_CHUNK, a["w_out_b"][0].rearrange("(k p) n -> p k n", p=P), (4, D))
            for i in range(2):
                front_chunk(O_CHUNK + i, a["w_o"][0, i * 512:(i + 1) * 512, :].rearrange("(k p) n -> p k n", p=P),
                            (4, D))
            wait_chunk_read(sp, 18)
            wait_chunk_read(sp, 19)
            sp.wait_ge(mod_stored, 16 * 12)
            sp.dma_start(ring[:, 0, 0:3 * D], mod_rows[0, 2 * D:5 * D].partition_broadcast(P)).then_inc(norm1_landed, 16)
            sp.dma_start(ring[:, 0, 3 * D:], a["ln1_g"][0].partition_broadcast(P)).then_inc(norm1_landed, 16)
            for s in range(NSEQ):
                sp.dma_start(ring[TSEQ * s:TSEQ * (s + 1), 1, 0:3 * D],
                             mod_rows[1 + s, 2 * D:5 * D].partition_broadcast(TSEQ)).then_inc(norm1_landed, 16)
            sp.dma_start(ring[:, 1, 3 * D:], a["ln1_b"][0].partition_broadcast(P)).then_inc(norm1_landed, 16)

            def expert_chunk(c, e):
                s = expert_slot(c)
                if c < 4:
                    j, half = divmod(c, 2)
                    for g in range(2):
                        src = a["w_up"][0][:, half * 512:(half + 1) * 512, g * D + j * 512:g * D + (j + 1) * 512]
                        sp.dma_start(ring[:, s, g * 2048:(g + 1) * 2048].rearrange("p (k m) -> p k m", k=4),
                                     src.rearrange("e (k p) m -> p e k m", p=P)[:, e]).then_inc(chunk_landed[s], 16)
                else:
                    src = a["w_down"][0][:, (c - 4) * 512:(c - 3) * 512, :].rearrange("e (k p) m -> p e k m", p=P)
                    sp.dma_start(ring[:, s, :].rearrange("p (k m) -> p k m", k=4), src[:, e]).then_inc(chunk_landed[s], 16)

            for c in range(EXPERT_CHUNKS):
                if expert_slot(c) < 2:
                    sp.wait_ge(v_ready, 3)
                else:
                    wait_chunk_read(sp, 18 + expert_slot(c))
                expert_chunk(c, 0)
            sp.wait_ge(table_ready, 1)
            ends_with = {1: B_UP[0], 3: B_UP[1], 5: B_DOWN}
            with sp.Fori(1, E) as e:
                rounds_done = sp.value_load(table[0:1, bass.ds(e + 127, 1)], min_val=1, max_val=52)
                for c in range(EXPERT_CHUNKS):
                    if c in ends_with:
                        b = ends_with[c]
                        sp.wait_ge(bank_full[b], rounds_done + front_uses(b))
                    else:
                        s = expert_slot(c)
                        sp.wait_ge(chunk_used[s], rounds_done + used_before(s))
                    expert_chunk(c, e)

        @block.gpsimd
        def _(pool):
            pool.dma_start(const[:, :], a["const"]).then_inc(const_landed, 16)
            pool.dma_start(c_rows[0:1, :], a["c_prompt"]).then_inc(rows_landed, 16)
            pool.dma_start(c_rows[1:NC_ROWS, :], a["c_sample"]).then_inc(rows_landed, 16)
            pool.dma_start(chan_rows[0:12, :], a["conv_w"][0].rearrange("j (b i) -> (j b) i", i=P)).then_inc(rows_landed, 16)
            pool.dma_start(chan_rows[12:16, :], a["ls_pool"][0].rearrange("(b i) -> b i", i=P)).then_inc(rows_landed, 16)
            for q in range(4):
                src = a["b_ada"][0].rearrange("(n q m) -> n q m", n=3, q=4)[:, q, :]
                pool.dma_start(b_ada_rows[32 * q:32 * q + NC_ROWS, :, :], src.partition_broadcast(NC_ROWS)).then_inc(bada_landed, 16)
            pool.dma_start(hx[:, 0:2, :], a["x_prompt"][0].rearrange("(t p) d -> p t d", p=P)).then_inc(x_landed, 16)
            pool.dma_start(hx[0:NS_TOK, 2, :], a["x_sample"].rearrange("s t d -> (s t) d")).then_inc(x_landed, 16)
            pool.dma_start(conv_hist[0:NSEQ * HIST_C, :], a["state_conv"][0].rearrange("s t d -> (s t) d")).then_inc(hist_landed, 16)
            pool.dma_start(pool_hist[0:NSEQ * HIST_P, :], a["state_pool"][0].rearrange("s t d -> (s t) d")).then_inc(hist_landed, 16)
            pool.dma_start(w_pool, a["w_pool"][0].rearrange("g c d -> c g d")).then_inc(pool_w_landed, 16)
            for name in ("state_cp", "state_cs", "state_pp", "state_ps"):
                wait_read(pool, name)
            rows = ((o["conv_p"][0, 0], 2, 0), (o["conv_s"][0].rearrange("s t d -> (s t) d"), 16, 1),
                    (o["pool_p"][0, 0], 15, 2), (o["pool_s"][0].rearrange("s t d -> (s t) d"), 120, 3))
            for dst, n, i in rows:
                pool.dma_start(dst, state_rows[0:n, i, :]).then_inc(out_stored, 16)
            for n in range(3):
                wait_read(pool, f"ada{n}")
                for q in range(4):
                    pool.dma_start(mod_rows[:, n * 2048 + q * 512:n * 2048 + (q + 1) * 512],
                                   mod[32 * q:32 * q + NC_ROWS, n, :]).then_inc(mod_stored, 16)
            wait_full(pool, "pool3")
            pool.dma_start(w_router, a["w_router"][0].rearrange("(k p) e -> p k e", p=P)).then_inc(router_landed, 16)
            pool.dma_start(b_router, a["b_router"][0].partition_broadcast(P)).then_inc(router_landed, 16)
            pool.wait_ge(mod_stored, 16 * 12)
            pool.dma_start(tail_rows[:, 0:D], mod_rows[0, 5 * D:].partition_broadcast(P)).then_inc(tail_landed, 16)
            for s in range(NSEQ):
                pool.dma_start(tail_rows[TSEQ * s:TSEQ * (s + 1), D:2 * D],
                               mod_rows[1 + s, 5 * D:].partition_broadcast(TSEQ)).then_inc(tail_landed, 16)
            pool.dma_start(tail_rows[:, 2 * D:3 * D], a["ln2_g"][0].partition_broadcast(P)).then_inc(tail_landed, 16)
            pool.dma_start(tail_rows[:, 3 * D:], a["ln2_b"][0].partition_broadcast(P)).then_inc(tail_landed, 16)
            wait_full(pool, "state_ps")
            pool.wait_ge(conv_ready, 4)
            for q in range(3):
                pool.dma_start(b_up_rows[32 * q:32 * q + E, :], a["b_up"][0]).then_inc(bias_landed, 16)
            done = [0]

            def part(ins):
                done[0] += 1
                ins.then_inc(parts_step, 1)
                pool.wait_ge(parts_step, done[0])

            part(pool.memset(b_up_parts, 0.0))
            pool.wait_ge(bias_landed, 48)
            for q in range(3):
                rows, parts = b_up_rows[32 * q:32 * q + E, :], b_up_parts[32 * q:32 * q + E, :]
                for i in range(q):
                    part(pool.tensor_copy(parts, rows))
                    part(pool.tensor_tensor(rows, rows, parts, ALU.subtract))
                part(pool.tensor_copy(parts, rows))
            pool.memset(b_up_rows[0:1, 0:1], 0.0).then_inc(b_up_ready, 1)
            pool.wait_ge(O_cleared, 1)
            pool.dma_start(O_rows[0:E, :, :], a["b_down"][0].rearrange("e (h m) -> e h m", h=2)).then_inc(b_down_landed, 16)
            outs = (o["y_p"][0, 0:P], o["y_p"][0, P:2 * P], o["y_s"].rearrange("s t d -> (s t) d"))
            for t in range(3):
                pool.wait_ge(y_ready, t + 1)
                pool.dma_start(outs[t], V[0:ROWS[t], t, :]).then_inc(out_stored, 16)
            pool.wait_ge(out_stored, 16 * 7)

        @block.tensor
        def _(pe):
            mm = nc.tensor.matmul

            def take(name):
                b, n = front_place(name)
                if n:
                    pe.wait_ge(bank_free[b], n)
                return bank[b]

            def done(name, ins):
                ins.then_inc(bank_full[front_place(name)[0]], 1)

            def chunk(n):
                s = front_slot(n)
                pe.wait_ge(chunk_landed[s], 16 * (n // RING + 1))
                return ring[:, s, :]

            pe.wait_ge(const_landed, 16)
            pe.wait_ge(rows_landed, 64)
            ps = take("c_T")
            for k in range(KC):
                last = nc.tensor.transpose(ps[:, k * NC_ROWS:(k + 1) * NC_ROWS], c_rows[0:NC_ROWS, k * P:(k + 1) * P],
                                           ident[0:NC_ROWS, 0:NC_ROWS])
            done("c_T", last)
            ps = take("chan_T")
            done("chan_T", nc.tensor.transpose(ps[:, 0:16], chan_rows[0:16, :], ident[0:16, 0:16]))

            def ada(third):
                ps = take(f"ada{third}")
                for i in range(4):
                    w = chunk(ADA_CHUNK[third] + i).rearrange("p (a b) -> p a b", a=2)
                    for kk in range(2):
                        k = 2 * i + kk
                        for q in range(4):
                            last = mm(ps[32 * q:32 * q + NC_ROWS, :], sc_T[:, k, :], w[:, kk, q * 512:(q + 1) * 512],
                                      start=k == 0, stop=k == KC - 1)
                    if i < 3:
                        last.then_inc(chunk_used[front_slot(ADA_CHUNK[third] + i)], 1)
                done(f"ada{third}", last)

            wait_read(pe, "c_T")
            ada(0)
            wait_read(pe, "ada0")
            ps = take("mod_T")
            for blk in range(4):
                last = nc.tensor.transpose(ps[:, blk * P:(blk + 1) * P], mod[:, 0, blk * P:(blk + 1) * P], ident)
            done("mod_T", last)
            pe.wait_ge(x_landed, 32)
            for k in range(KC):
                ps = take(f"x_T{k}")
                for t in range(3):
                    r = ROWS[t]
                    last = nc.tensor.transpose(ps[:, t * P:t * P + r], hx[0:r, t, k * P:(k + 1) * P], ident[0:r, 0:r])
                done(f"x_T{k}", last)
            pe.wait_ge(hist_landed, 32)
            for name, src, r in (("conv_hist_T", conv_hist, 16), ("pool_hist_T", pool_hist, 120)):
                ps = take(name)
                for blk in range(4):
                    last = nc.tensor.transpose(ps[:, blk * r:(blk + 1) * r], src[0:r, blk * P:(blk + 1) * P], ident[0:r, 0:r])
                done(name, last)

            def proj(i, m4):
                w = chunk(IN_CHUNK + i).rearrange("p (k m) -> p k m", k=KC)
                for j in range(4):
                    name = f"proj{4 * m4 + j}"
                    ps = take(name)
                    for k in range(KC):
                        if i == 0 and j == 0:
                            wait_read(pe, f"x_T{k}")
                        last = mm(ps[:, 0:NT], w[:, k, j * P:(j + 1) * P], u_T[:, k, :], start=k == 0, stop=k == KC - 1)
                    done(name, last)

            for i in range(8):
                proj(i, IN_ORDER[i])
            pe.wait_ge(pool_w_landed, 16)
            for g in range(4):
                pe.wait_ge(diff_ready, g + 1)
                ps = take(f"pool{g}")
                done(f"pool{g}", mm(ps[:, 0:NT], w_pool[:, g, :], diff_T[:, g, :], start=True, stop=True))

            pe.wait_ge(keep_ready, 2)
            pieces = (("state_cp", 2, lambda b: z_p[:, b, NP_TOK:]),
                      ("state_cs", 16, lambda b: keep_s[:, b, :, :].rearrange("p s t -> p (s t)")),
                      ("state_pp", 15, lambda b: pool_p[:, b, NP_TOK:]),
                      ("state_ps", 120, lambda b: keep_ps[:, b, :, :].rearrange("p s t -> p (s t)")))
            for name, r, piece in pieces:
                ps = take(name)
                for b in range(4):
                    last = nc.tensor.transpose(ps[0:r, b * P:(b + 1) * P], piece(b), ident)
                done(name, last)
            ada(1)
            ada(2)
            pe.wait_ge(conv_ready, 4)
            w = chunk(OUTA_CHUNK).rearrange("p (k m) -> p k m", k=4)
            for m in range(8):
                ps = take(f"out_a{m}")
                for k in range(4):
                    last = mm(ps[:, 0:NT], w[:, k, m * P:(m + 1) * P], y_in_T[:, k, :], start=k == 0, stop=k == 3)
                done(f"out_a{m}", last)
            for g in range(4):
                wait_read(pe, f"pool{g}")
            w = chunk(OUTB_CHUNK).rearrange("p (k m) -> p k m", k=4)
            for m in range(8):
                ps = take(f"out_b{m}")
                for k in range(4):
                    last = mm(ps[:, 0:NT], w[:, k, m * P:(m + 1) * P], yg_T[:, k, :], start=k == 0, stop=k == 3)
                done(f"out_b{m}", last)
            wo = [chunk(O_CHUNK + i).rearrange("p (k m) -> p k m", k=4) for i in range(2)]
            for t in range(3):
                r = ROWS[t]
                for h in range(2):
                    ps = take(f"o{t}{h}")
                    for k in range(KC):
                        if t == 0 and h == 0:
                            wait_read(pe, f"out_b{k}")
                        last = mm(ps[0:r, :], ga_T[:, k, t * P:t * P + r], wo[k // 4][:, k % 4, h * 512:(h + 1) * 512],
                                  start=k == 0, stop=k == KC - 1)
                        if k == 3 and t == 2 and h == 1:
                            last.then_inc(chunk_used[front_slot(O_CHUNK)], 1)
                    done(f"o{t}{h}", last)
            pe.wait_ge(v_ready, 3)
            for k in range(KC):
                ps = take(f"v_T{k}")
                for t in range(3):
                    r = ROWS[t]
                    last = nc.tensor.transpose(ps[:, t * P:t * P + r], V[0:r, t, k * P:(k + 1) * P], ident[0:r, 0:r])
                done(f"v_T{k}", last)
            pe.wait_ge(router_landed, 32)
            for k in range(KC):
                wait_read(pe, f"v_T{k}")
            ps = take("logits")
            for t in range(3):
                for k in range(KC):
                    last = mm(ps[0:ROWS[t], t * E:(t + 1) * E], v_T[:, k, t * P:t * P + ROWS[t]], w_router[:, k, :],
                              start=k == 0, stop=k == KC - 1)
            done("logits", last)
            pe.wait_ge(mask_ready, 1)
            ps = take("rank")
            for t in range(3):
                for i in range(t + 1):
                    lhs = tri if i == t else ones
                    last = mm(ps[0:ROWS[t], t * E:(t + 1) * E], lhs[0:ROWS[i], 0:ROWS[t]], mask[0:ROWS[i], i, :],
                              start=i == 0, stop=i == t)
            done("rank", last)
            ps = take("counts")
            for t in range(3):
                last = mm(ps[0:E, 0:1], mask[0:ROWS[t], t, :], ones[0:ROWS[t], 0:1], start=t == 0, stop=t == 2)
            done("counts", last)
            pe.wait_ge(rounds_ready, 1)
            ps = take("bounds")
            done("bounds", mm(ps[0:E, 0:1], tri_incl[0:E, :], rounds[0:E, :], start=True, stop=True))
            pe.wait_ge(passed_ready, 1)
            ps = take("table")
            mm(ps[0:1, 0:NROUND], ones[0:E, 0:1], passed[0:E, :], start=True, stop=True)
            mm(ps[0:1, NROUND:2 * NROUND], rounds[0:E, :], passed[0:E, :], start=True, stop=True)
            done("table", mm(ps[0:1, 2 * NROUND:2 * NROUND + E], rounds[0:E, :], tri_incl[0:E, :], start=True, stop=True))

            pe.wait_ge(softmax_ready, 1)
            ps = take("gate_T")
            for t in range(3):
                r = ROWS[t]
                last = nc.tensor.transpose(ps[0:E, t * P:t * P + r], gate[0:r, t, :], ident[0:r, 0:r])
            done("gate_T", last)

            def gather(n, x_rows_read=None):
                pe.wait_ge(S_ready, n + 1)
                if x_rows_read is not None:
                    pe.wait_ge(x_rows_ready, x_rows_read)
                for t in range(3):
                    for h in range(2):
                        last = mm(bank[B_X][64 * h:64 * h + 64, :], S[0:ROWS[t], t, :], V[0:ROWS[t], t, h * 512:(h + 1) * 512],
                                  start=t == 0, stop=t == 2)
                last.then_inc(bank_full[B_X], 1)

            def x_transposes(n, xT_read=None):
                pe.wait_ge(x_rows_ready, n + 1)
                if xT_read is not None:
                    pe.wait_ge(xT_ready, xT_read)
                for q in range(4):
                    last = nc.tensor.transpose(bank[B_XT][:, q * P:(q + 1) * P], x_rows[:, q * P:(q + 1) * P], ident)
                last.then_inc(bank_full[B_XT], 1)

            def combine(n, pieces):
                for i in pieces:
                    b = COMBINE_BANKS[i]
                    if i == 0:
                        pe.wait_ge(O_ready, 2 * n + 2)
                        pe.wait_ge(Pg_ready, n + 1)
                    pe.wait_ge(bank_free[b], front_uses(b) + PER_ROUND[b] * n + COMBINE_BANKS[:i].count(b))
                    if i < 4:
                        t, h = divmod(i, 2)
                        last = mm(bank[b][:, :], P_gate[:, t * P:(t + 1) * P], O_rows[:, h, :], start=True, stop=True)
                    else:
                        for h in range(2):
                            last = mm(bank[b][64 * h:64 * h + 64, :], P_gate[:, 2 * P:NT], O_rows[:, h, :],
                                      start=True, stop=True)
                    last.then_inc(bank_full[b], 1)

            pe.wait_ge(table_ready, 1)
            G = pe.value_load(table[0:1, 159:160], min_val=1, max_val=52)
            gather(0)
            x_transposes(0)
            pe.wait_ge(b_up_ready, 1)
            with pe.Fori(0, G) as g:
                e = pe.value_load(table[0:1, bass.ds(g, 1)], min_val=0, max_val=E - 1)
                for j in range(2):
                    b = B_UP[j]
                    pe.wait_ge(bank_free[b], g + front_uses(b))
                    if j == 0:
                        pe.wait_ge(sel_ready, g + 1)
                    for h in range(2):
                        at = j * 512 + h * 256
                        mm(bank[b][64 * h:64 * h + 64, :], up_sel,
                           b_up_parts.rearrange("p (g m) -> p g m", g=2)[:, :, at:at + 256], start=True, stop=False)
                    if j == 0:
                        pe.wait_ge(xT_ready, g + 1)
                    for k in range(KC):
                        s = expert_slot(2 * j + k // 4)
                        if k % 4 == 0:
                            pe.wait_ge(chunk_landed[s], e * 32 + 16 * landed_before(s) + 32)
                        w = ring[:, s, :].rearrange("p (g k m) -> p g k m", g=2, k=4)[:, :, k % 4, :]
                        for h in range(2):
                            last = mm(bank[b][64 * h:64 * h + 64, :], x_T[:, k % 4, 64 * (k // 4):64 * (k // 4) + 64],
                                      w[:, :, h * 256:(h + 1) * 256], start=False, stop=k == KC - 1)
                        if k == 3:
                            last.then_inc(chunk_used[s], 1)
                    last.then_inc(bank_full[b], 1)
                gather(g + 1, x_rows_read=g + 1)
                combine(g, (0, 1, 2))
                pe.wait_ge(act_ready, 2 * g + 2)
                pe.wait_ge(Pg_ready, g + 1)
                for q in range(4):
                    last = nc.tensor.transpose(bank[B_T][:, q * P:(q + 1) * P], act_rows[:, q * P:(q + 1) * P], ident)
                last.then_inc(bank_full[B_T], 1)
                x_transposes(g + 1, xT_read=g + 1)
                combine(g, (3, 4))
                pe.wait_ge(gate_ready, g + 1)
                pe.wait_ge(actT_ready, g + 1)
                for t in range(3):
                    r = ROWS[t]
                    last = nc.tensor.transpose(bank[B_T][:, t * P:t * P + r], S_gate[0:r, t, :], ident[0:r, 0:r])
                last.then_inc(bank_full[B_T], 1)
                for k in range(KC):
                    s = expert_slot(4 + k // 4)
                    if k % 4 == 0:
                        pe.wait_ge(chunk_landed[s], e * 16 + 16 * landed_before(s) + 16)
                    q, hh = 2 * (k // 4) + k % 2, (k % 4) // 2
                    for h in range(2):
                        last = mm(bank[B_DOWN][64 * h:64 * h + 64, :], act_T[:, q, 64 * hh:64 * hh + 64],
                                  ring[:, s, (k % 4) * 1024 + h * 512:(k % 4) * 1024 + (h + 1) * 512], start=k == 0, stop=k == KC - 1)
                    if k == 3:
                        last.then_inc(chunk_used[s], 1)
                last.then_inc(bank_full[B_DOWN], 1)
            combine(G, range(5))

        @block.scalar
        def _(act):
            AF = nc.scalar.activation

            def free(name, ins):
                ins.then_inc(bank_free[front_place(name)[0]], 1)

            ps = wait_full(act, "c_T")
            AF(sg_c, ps[:, 0:KC * NC_ROWS].rearrange("p (k b) -> p k b", k=KC), ACT.Sigmoid).then_inc(c_sig_ready, 1)
            for m in (4, 5, 6, 7):
                ps = wait_full(act, f"proj{m}")
                free(f"proj{m}", AF(c_T[:, m - 4, :], ps[:, 0:NT], ACT.Copy))
            for m in range(4):
                ps = wait_full(act, f"proj{m}")
                free(f"proj{m}", AF(b_T[:, m, :], ps[:, 0:NT], ACT.Copy))
            for m in range(16, 32):
                ps = wait_full(act, f"proj{m}")
                dst = ga_T if m < 24 else gb_T
                free(f"proj{m}", AF(dst[:, (m - 16) % 8, :], ps[:, 0:NT], ACT.Sigmoid))
            for i, (name, r) in enumerate((("state_cp", 2), ("state_cs", 16), ("state_pp", 15), ("state_ps", 120))):
                ps = wait_full(act, name)
                free(name, AF(state_rows[0:r, i, :], ps[0:r, :], ACT.Copy))
            def root(n):
                r = ROWS[n % 3]
                act.wait_ge(var_ready, n + 1)
                AF(rstd[0:r, :], aggr[0:r, 1:2], ACT.Sqrt).then_inc(sqrt_ready, 1)

            for n in range(3):
                root(n)
            for k in range(KC):
                ps = wait_full(act, f"v_T{k}")
                free(f"v_T{k}", AF(v_T[:, k, :], ps[:, 0:NT], ACT.Copy))
            act.wait_ge(logit_ready, 1)
            AF(gate[:, :, :], eq[:, :, :], ACT.Exp).then_inc(exp_ready, 1)

            def x_copy(n):
                act.wait_ge(bank_full[B_X], front_uses(B_X) + n + 1)
                AF(x_rows[:, :], bank[B_X][:, :], ACT.Copy).then_inc(x_rows_ready, 1)

            def xT_copy(n):
                act.wait_ge(bank_full[B_XT], front_uses(B_XT) + n + 1)
                AF(x_T[:, :, :], bank[B_XT][:, :].rearrange("p (q s) -> p q s", q=4), ACT.Copy).then_inc(xT_ready, 1)

            act.wait_ge(table_ready, 1)
            G = act.value_load(table[0:1, 159:160], min_val=1, max_val=52)
            x_copy(0)
            xT_copy(0)
            with act.Fori(0, G) as g:
                for j in range(2):
                    act.wait_ge(glu_ready, 2 * g + j + 1)
                    AF(sig[:, j, :], glu[:, j, :], ACT.Sigmoid, scale=SWISH).then_inc(sig_ready, 1)
                x_copy(g + 1)
                act.wait_ge(bank_full[B_T], front_uses(B_T) + 2 * g + 1)
                AF(act_T[:, :, :], bank[B_T][:, :].rearrange("p (q s) -> p q s", q=4), ACT.Copy).then_inc(actT_ready, 1)
                xT_copy(g + 1)
                act.wait_ge(bank_full[B_T], front_uses(B_T) + 2 * g + 2)
                AF(P_gate[0:SLOTS, :], bank[B_T][0:SLOTS, 0:NT], ACT.Copy).then_inc(Pg_ready, 1)
                act.wait_ge(bank_full[B_DOWN], g + front_uses(B_DOWN) + 1)
                for h in range(2):
                    AF(O_rows[0:SLOTS, h, :], bank[B_DOWN][64 * h:64 * h + 64, :], ACT.Copy).then_inc(O_ready, 1)
            for n in range(3, 6):
                root(n)

        @block.vector
        def _(dve):
            v = nc.vector
            steps = [0]
            origin = [0]
            step_sem = [dve_step]

            def step(ins):
                steps[0] += 1
                ins.then_inc(step_sem[0], 1)
                dve.wait_ge(step_sem[0], origin[0] + steps[0])

            def signal(ins, sem, value):
                ins.then_inc(sem, 1)
                dve.wait_ge(sem, value)

            def free(name, ins):
                b, n = front_place(name)
                signal(ins, bank_free[b], n + 1)

            TS, TT, STT = v.tensor_scalar, v.tensor_tensor, v.scalar_tensor_tensor
            step(v.memset(mod[:, 0, :], 0.0))
            step(v.memset(z_p[:, :, 0:HIST_C], 0.0))
            step(v.memset(pool_p[:, :, 0:HIST_P], 0.0))
            dve.wait_ge(c_sig_ready, 1)
            ps = wait_full(dve, "c_T")
            free("c_T", TT(sc_T, ps[:, 0:KC * NC_ROWS].rearrange("p (k b) -> p k b", k=KC), sg_c, ALU.mult))
            ps = wait_full(dve, "chan_T")
            free("chan_T", v.tensor_copy(chan, ps[:, 0:16]))
            dve.wait_ge(bada_landed, 64)

            def ada(third):
                ps = wait_full(dve, f"ada{third}")
                for q in range(4):
                    r = slice(32 * q, 32 * q + NC_ROWS)
                    ins = TT(mod[r, third, :], ps[r, :], b_ada_rows[r, third, :], ALU.add)
                    if q < 3:
                        step(ins)
                    else:
                        free(f"ada{third}", ins)

            ada(0)
            ps = wait_full(dve, "mod_T")[:, :].rearrange("p (b r) -> p b r", b=4)
            step(v.tensor_copy(mod_T[:, :, 0:64], ps[:, :, 0:64]))
            free("mod_T", TS(mod_T[:, :, 64:P], ps[:, :, 64:P], 1.0, None, ALU.add))
            for k in range(KC):
                ps = wait_full(dve, f"x_T{k}")
                q, blk = divmod(k, 4)
                sh, sc = mod_T[:, blk, 32 * q:32 * q + NC_ROWS], mod_T[:, blk, 32 * q + 64:32 * q + 64 + NC_ROWS]
                by_seq = lambda t: t.rearrange("p (s t) -> p s t", s=NSEQ)
                wide = lambda t: t[:, 1:NC_ROWS].unsqueeze(2).to_broadcast([P, NSEQ, TSEQ])
                step(TS(u_T[:, k, 0:NP_TOK], ps[:, 0:NP_TOK], sc[:, 0:1], sh[:, 0:1], ALU.mult, ALU.add))
                step(TT(by_seq(u_T[:, k, NP_TOK:]), by_seq(ps[:, NP_TOK:NT]), wide(sc), ALU.mult))
                free(f"x_T{k}", TT(by_seq(u_T[:, k, NP_TOK:]), by_seq(u_T[:, k, NP_TOK:]), wide(sh), ALU.add))
            ps = wait_full(dve, "conv_hist_T")
            free("conv_hist_T", v.tensor_copy(z_s[:, :, :, 0:HIST_C], ps[:, 0:64].rearrange("p (b s t) -> p b s t", b=4, s=NSEQ)))
            ps = wait_full(dve, "pool_hist_T")
            free("pool_hist_T", v.tensor_copy(pool_s[:, :, :, 0:HIST_P], ps[:, 0:480].rearrange("p (b s t) -> p b s t", b=4, s=NSEQ)))
            for b in range(4):
                ps = wait_full(dve, f"proj{8 + b}")
                wait_read(dve, f"proj{4 + b}")
                step(TT(z_p[:, b, HIST_C:], ps[:, 0:NP_TOK], c_T[:, b, 0:NP_TOK], ALU.mult))
                free(f"proj{8 + b}", TT(z_s[:, b, :, HIST_C:], by_seq(ps[:, NP_TOK:NT]), by_seq(c_T[:, b, NP_TOK:]), ALU.mult))
            for b in range(4):
                ps = wait_full(dve, f"proj{12 + b}")
                step(v.tensor_copy(pool_p[:, b, HIST_P:], ps[:, 0:NP_TOK]))
                free(f"proj{12 + b}", v.tensor_copy(pool_s[:, b, :, HIST_P:], by_seq(ps[:, NP_TOK:NT])))
            signal(v.tensor_copy(keep_s, z_s[:, :, :, TSEQ:]), keep_ready, 1)
            signal(v.tensor_copy(keep_ps, pool_s[:, :, :, TSEQ:]), keep_ready, 2)
            for g, w in enumerate(WINDOWS):
                src_p, src_s = pool_p[:, g, :], pool_s[:, g, :, :]
                reach, n = 1, 0
                while reach < w:
                    dp, ds_ = sum_p[:, n % 2, :], sum_s[:, n % 2, :, :]
                    lo = 2 * reach - 1
                    step(TT(dp[:, lo:], src_p[:, lo:], src_p[:, lo - reach:HIST_P + NP_TOK - reach], ALU.add))
                    step(TT(ds_[:, :, lo:], src_s[:, :, lo:], src_s[:, :, lo - reach:HIST_P + TSEQ - reach], ALU.add))
                    src_p, src_s = dp, ds_
                    reach, n = 2 * reach, n + 1
                step(STT(diff_T[:, g, 0:NP_TOK], src_p[:, HIST_P:], 1.0 / w, pool_p[:, g, HIST_P:], ALU.mult, ALU.subtract))
                step(TT(diff_T[:, g, 0:HIST_P], src_p[:, HIST_P:2 * HIST_P], inv_count[:, g, :], ALU.mult))
                step(TT(diff_T[:, g, 0:HIST_P], diff_T[:, g, 0:HIST_P], pool_p[:, g, HIST_P:2 * HIST_P], ALU.subtract))
                signal(STT(by_seq(diff_T[:, g, NP_TOK:]), src_s[:, :, HIST_P:], 1.0 / w, pool_s[:, g, :, HIST_P:],
                           ALU.mult, ALU.subtract), diff_ready, g + 1)
            for b in range(4):
                wait_read(dve, f"proj{b}")
                yp, ys = y_in_T[:, b, 0:NP_TOK], by_seq(y_in_T[:, b, NP_TOK:])
                tap = lambda j: chan[:, 4 * j + b:4 * j + b + 1]
                step(TS(yp, z_p[:, b, 0:NP_TOK], tap(0), None, ALU.mult))
                step(TS(ys, z_s[:, b, :, 0:TSEQ], tap(0), None, ALU.mult))
                for j in (1, 2):
                    step(STT(yp, z_p[:, b, j:j + NP_TOK], tap(j), yp, ALU.mult, ALU.add))
                    step(STT(ys, z_s[:, b, :, j:j + TSEQ], tap(j), ys, ALU.mult, ALU.add))
                signal(TT(y_in_T[:, b, :], y_in_T[:, b, :], b_T[:, b, :], ALU.mult), conv_ready, b + 1)
            for g in range(4):
                ps = wait_full(dve, f"pool{g}")
                free(f"pool{g}", TS(yg_T[:, g, :], ps[:, 0:NT], chan[:, 12 + g:13 + g], None, ALU.mult))
            ada(1)
            ada(2)
            for m in range(KC):
                ps = wait_full(dve, f"out_a{m}")
                wait_read(dve, f"proj{16 + m}")
                free(f"out_a{m}", TT(ga_T[:, m, :], ga_T[:, m, :], ps[:, 0:NT], ALU.mult))
            for m in range(KC):
                ps = wait_full(dve, f"out_b{m}")
                wait_read(dve, f"proj{24 + m}")
                step(TT(gb_T[:, m, :], gb_T[:, m, :], ps[:, 0:NT], ALU.mult))
                free(f"out_b{m}", TT(ga_T[:, m, :], ga_T[:, m, :], gb_T[:, m, :], ALU.add))
            step(v.memset(Y, 0.0))

            normed = [0]

            def normalise(dst, row, gain, offset, last):
                r = row.shape[0]
                step(v.bn_stats(stats[0:r, 0:6], row[:, 0:512]))
                step(v.bn_stats(stats[0:r, 6:12], row[:, 512:]))
                step(v.bn_aggr(aggr[0:r, :], stats[0:r, :]))
                normed[0] += 1
                signal(TS(aggr[0:r, 1:2], aggr[0:r, 1:2], EPS, None, ALU.add), var_ready, normed[0])
                dve.wait_ge(sqrt_ready, normed[0])
                step(v.reciprocal(rstd[0:r, :], rstd[0:r, :]))
                step(TT(rstd2[0:r, :], rstd[0:r, :], rstd[0:r, :], ALU.mult))
                step(TT(rstd2[0:r, :], rstd2[0:r, :], aggr[0:r, 1:2], ALU.mult))
                step(TS(rstd2[0:r, :], rstd2[0:r, :], -0.5, 1.5, ALU.mult, ALU.add))
                step(TT(rstd[0:r, :], rstd[0:r, :], rstd2[0:r, :], ALU.mult))
                step(TS(row, row, aggr[0:r, 0:1], rstd[0:r, :], ALU.subtract, ALU.mult))
                step(TT(row, row, gain, ALU.mult))
                last(TT(dst, row, offset, ALU.add))

            dve.wait_ge(norm1_landed, 16 * (3 + NSEQ))
            dve.wait_ge(out_stored, 64)
            for t in range(3):
                r = ROWS[t]
                vec = ring[0:r, 0 if t < 2 else 1, 0:3 * D].rearrange("p (i d) -> p i d", i=3)
                row = ln_rows[0:r, :]
                for h in range(2):
                    ps = wait_full(dve, f"o{t}{h}")
                    free(f"o{t}{h}", TT(row[:, h * 512:(h + 1) * 512], ps[0:r, :], vec[:, 0, h * 512:(h + 1) * 512], ALU.mult))
                step(STT(row, hx[0:r, t, :], ALPHA, row, ALU.mult, ALU.add))
                normalise(hx[0:r, t, :], row, ring[0:r, 0, 3 * D:], ring[0:r, 1, 3 * D:], step)
                step(STT(V[0:r, t, :], vec[:, 2, :], 1.0, hx[0:r, t, :], ALU.add, ALU.mult))
                signal(TT(V[0:r, t, :], V[0:r, t, :], vec[:, 1, :], ALU.add), v_ready, t + 1)

            signal(v.memset(O_rows, 0.0), O_cleared, 1)
            dve.wait_ge(router_landed, 32)
            step(v.memset(L, 0.0))
            step(v.memset(top, 0.0))
            step(v.memset(top_f, 0.0))
            ps = wait_full(dve, "logits")
            for t in range(3):
                r = ROWS[t]
                ins = TT(L[0:r, t, :], ps[0:r, t * E:(t + 1) * E], b_router[0:r, :], ALU.add)
                step(ins) if t < 2 else free("logits", ins)
            for t in range(3):
                r = ROWS[t]
                step(v.max(top[0:r, t, :], L[0:r, t, :]))
                step(v.max_index(top_index[0:r, t, :], top[0:r, t, :], L[0:r, t, :]))
                step(v.tensor_copy(top_f[0:r, t, :], top_index[0:r, t, :]))
            by_e = lambda t: t.to_broadcast([P, 3, E])
            experts = iota[:, 0:E].unsqueeze(1).to_broadcast([P, 3, E])
            signal(TT(eq, L, by_e(top[:, :, 0:1]), ALU.subtract), logit_ready, 1)
            step(TT(mask, experts, by_e(top_f[:, :, 0:1]), ALU.is_equal))
            dve.wait_ge(exp_ready, 1)
            for k in range(1, TOPK):
                step(TT(eq, experts, by_e(top_f[:, :, k:k + 1]), ALU.is_equal))
                ins = TT(mask, mask, eq, ALU.add)
                step(ins) if k < TOPK - 1 else signal(ins, mask_ready, 1)
            step(TT(gate, gate, mask, ALU.mult))
            step(v.reduce_sum(gsum, gate, AX_X))
            step(v.reciprocal(gsum, gsum))
            signal(TT(gate, gate, by_e(gsum.unsqueeze(2)), ALU.mult), softmax_ready, 1)
            ps = wait_full(dve, "rank")
            step(v.memset(rank, -1.0))
            for t in range(3):
                r = ROWS[t]
                ins = STT(rank[0:r, t, :], ps[0:r, t * E:(t + 1) * E], 1.0, mask[0:r, t, :], ALU.add, ALU.mult)
                step(ins) if t < 2 else free("rank", ins)
            for t in range(3):
                step(TS(rank[0:ROWS[t], t, :], rank[0:ROWS[t], t, :], -1.0, None, ALU.add))
            ps = wait_full(dve, "counts")
            free("counts", v.tensor_copy(count[0:E, :], ps[0:E, 0:1]))
            step(TS(rounds[0:E, :], count[0:E, :], float(SLOTS), 1.0, ALU.is_gt, ALU.add))
            for i in range(2, MAXR):
                ins = STT(rounds[0:E, :], count[0:E, :], float(i * SLOTS), rounds[0:E, :], ALU.is_gt, ALU.add)
                step(ins) if i < MAXR - 1 else signal(ins, rounds_ready, 1)
            ps = wait_full(dve, "bounds")
            free("bounds", v.tensor_copy(bound[0:E, :], ps[0:E, 0:1]))
            signal(TS(passed[0:E, :], iota[0:E, 0:NROUND], bound[0:E, :], None, ALU.is_ge), passed_ready, 1)
            ps = wait_full(dve, "table")
            step(TS(table[0:1, 0:NROUND], ps[0:1, 0:NROUND], float(E - 1), None, ALU.min))
            step(TT(base_f[0:1, :], iota[0:1, 0:NROUND], ps[0:1, NROUND:2 * NROUND], ALU.subtract))
            step(TS(table[0:1, NROUND:2 * NROUND], base_f[0:1, :], float(SLOTS), None, ALU.mult))
            free("table", v.tensor_copy(table[0:1, 2 * NROUND:2 * NROUND + E], ps[0:1, 2 * NROUND:2 * NROUND + E]))
            step(v.memset(S_gate, 0.0))
            step(v.memset(P_gate, 0.0))
            signal(v.memset(stats[0:1, 0:1], 0.0), table_ready, 1)
            ps = wait_full(dve, "gate_T")
            free("gate_T", v.tensor_copy(P_gate[0:E, :], ps[0:E, 0:NT]))
            dve.wait_ge(b_down_landed, 16)
            signal(v.memset(stats[0:1, 0:1], 0.0), Pg_ready, 1)
            signal(v.memset(stats[0:1, 0:1], 0.0), O_ready, 1)
            signal(v.memset(stats[0:1, 0:1], 0.0), O_ready, 2)

            G = dve.value_load(table[0:1, 159:160], min_val=1, max_val=52)

            by_slot = lambda t: t.to_broadcast([P, 3, SLOTS])

            def one_hots(n, e, base):
                slots = iota[:, bass.ds(base, SLOTS)].unsqueeze(1).to_broadcast([P, 3, SLOTS])
                signal(TT(S, slots, by_slot(rank[:, :, bass.ds(e, 1)]), ALU.is_equal), S_ready, n + 1)

            def select_bias(n, e):
                signal(v.tensor_copy(up_sel, sel3[:, bass.ds(e, 1)].to_broadcast([P, SLOTS])), sel_ready, n + 1)

            def gated(n, e):
                signal(TT(S_gate[:, :, 0:SLOTS], S, by_slot(gate[:, :, bass.ds(e, 1)]), ALU.mult), gate_ready, n + 1)

            def add_up(n):
                used = {6: 0, 7: 0}
                for i, b in enumerate(COMBINE_BANKS):
                    used[b] += 1
                    value = front_uses(b) + PER_ROUND[b] * n + used[b]
                    dve.wait_ge(bank_full[b], value)
                    signal(TT(Y[:, i, :], Y[:, i, :], bank[b][:, :], ALU.add), bank_free[b], value)

            e0 = dve.value_load(table[0:1, 0:1], min_val=0, max_val=E - 1)
            one_hots(0, e0, 0)
            select_bias(0, e0)
            gated(0, e0)
            before = steps[0]
            PER_LOOP = 2
            with dve.Fori(0, G) as g:
                steps[0] = 0
                origin[0] = g * PER_LOOP + before
                e = dve.value_load(table[0:1, bass.ds(g + 1, 1)], min_val=0, max_val=E - 1)
                base = dve.value_load(table[0:1, bass.ds(g + NROUND + 1, 1)], min_val=0, max_val=(MAXR - 1) * SLOTS)
                dve.wait_ge(bank_full[B_X], g + front_uses(B_X) + 1)
                one_hots(g + 1, e, base)
                for j in range(2):
                    b = B_UP[j]
                    dve.wait_ge(bank_full[b], g + front_uses(b) + 1)
                    signal(TS(glu[:, j, :], bank[b][:, 0:256], LIMIT, None, ALU.min), glu_ready, 2 * g + j + 1)
                    signal(TS(lin[:, j, :], bank[b][:, 256:512], -LIMIT, LIMIT, ALU.max, ALU.min), bank_free[b],
                           g + front_uses(b) + 1)
                    step(STT(lin[:, j, :], lin[:, j, :], 1.0, glu[:, j, :], ALU.add, ALU.mult))
                    dve.wait_ge(sig_ready, 2 * g + j + 1)
                    signal(TT(act_rows[:, j * 256:(j + 1) * 256], lin[:, j, :], sig[:, j, :], ALU.mult), act_ready, 2 * g + j + 1)
                select_bias(g + 1, e)
                add_up(g)
                dve.wait_ge(bank_full[B_T], g * 2 + front_uses(B_T) + 2)
                gated(g + 1, e)
                assert steps[0] == PER_LOOP
            add_up(G)
            steps[0], origin[0], step_sem[0] = 0, 0, tail_step

            dve.wait_ge(tail_landed, 16 * (3 + NSEQ))
            step(v.tensor_copy(y2_rows[0:NS_TOK, :], Y[64:P, 4, :]))
            for t in range(3):
                r = ROWS[t]
                row = V[0:r, t, :]
                for h in range(2):
                    f = Y[0:r, 2 * t + h, :] if t < 2 else (Y[0:r, 4, :], y2_rows[0:r, :])[h]
                    at = (0 if t < 2 else D) + h * 512
                    step(TT(row[:, h * 512:(h + 1) * 512], f, tail_rows[0:r, at:at + 512], ALU.mult))
                step(STT(row, hx[0:r, t, :], ALPHA, row, ALU.mult, ALU.add))
                normalise(row, row, tail_rows[0:r, 2 * D:3 * D], tail_rows[0:r, 3 * D:], lambda ins, t=t: signal(ins, y_ready, t + 1))


INPUTS = ["x_prompt", "x_sample", "c_prompt", "c_sample", "state_conv", "state_pool", "w_ada", "b_ada", "w_in",
          "conv_w", "w_out_a", "w_pool", "ls_pool", "w_out_b", "w_o", "ln1_g", "ln1_b", "w_router", "b_router",
          "w_up", "b_up", "w_down", "b_down", "ln2_g", "ln2_b"]
OUTPUTS = {"y_p": (1, NP_TOK, D), "y_s": (NSEQ, TSEQ, D), "conv_p": (1, 1, HIST_C, DC), "pool_p": (1, 1, HIST_P, DC),
           "conv_s": (1, NSEQ, HIST_C, DC), "pool_s": (1, NSEQ, HIST_P, DC)}


def constants():
    c = np.zeros((P, C_N), np.float32)
    c[:, C_ID:C_ID + P] = np.eye(P)
    c[:, C_TRI:C_TRI + P] = np.triu(np.ones((P, P)), 1)
    c[:, C_ONE:C_ONE + P] = 1.0
    c[:, C_TRI1:C_TRI1 + E] = np.triu(np.ones((P, E)))
    c[:, C_IOTA:C_IOTA + NT] = np.arange(NT)
    for g, w in enumerate(WINDOWS):
        c[:, C_INV + g * HIST_P:C_INV + (g + 1) * HIST_P] = 1.0 / np.minimum(w, np.arange(HIST_P) + 1)
    for q in range(3):
        c[32 * q:32 * q + E, C_SEL:C_SEL + E] = np.eye(E)
    return c


def kernel(**inputs):
    import concourse.bacc as bacc
    from concourse.bass_utils import run_bass_kernel_spmd

    nc = bacc.Bacc("TRN2", target_bir_lowering=False, num_devices=1)
    arrays = {f"in_{n}": np.ascontiguousarray(inputs[n]) for n in INPUTS}
    arrays["in_const"] = constants()
    a = {n: nc.dram_tensor(f"in_{n}", arrays[f"in_{n}"].shape, F32, kind="ExternalInput").ap() for n in INPUTS + ["const"]}
    o = {n: nc.dram_tensor(f"out_{n}", shape, F32, kind="ExternalOutput").ap() for n, shape in OUTPUTS.items()}
    program(nc, a, o)
    r = run_bass_kernel_spmd(nc, [arrays], core_ids=[0]).results[0]
    return tuple(r[f"out_{n}"] for n in OUTPUTS)
```

```python
from contextlib import ExitStack

import numpy as np

import concourse.bass as bass
from concourse import mybir

F32R = mybir.dt.float32r
F32 = mybir.dt.float32
BF16 = mybir.dt.bfloat16
I32 = mybir.dt.int32
U32 = mybir.dt.uint32
ALU = mybir.AluOpType
ACT = mybir.ActivationFunctionType
AX_X = mybir.AxisListType.X

P = 128
D = 1024
DC = 512
KC = D // P
NP_TOK = 256
NSEQ, TSEQ = 8, 8
NS_TOK = NSEQ * TSEQ
NT = NP_TOK + NS_TOK
ROWS = (P, P, NS_TOK)
NC_ROWS = 1 + NSEQ
HIST_C, HIST_P = 2, 15
WINDOWS = (2, 4, 8, 16)
E = 32
TOPK = 4
SLOTS = 64
MAXR = -(-NT // SLOTS)
NROUND = 64
LIMIT, SWISH = 7.0, 1.702
EPS = 1e-5
ALPHA = 2.0 ** 0.25

C_ID, C_TRI, C_ONE, C_TRI1, C_IOTA, C_INV = 0, 128, 256, 384, 416, 736
C_SEL = C_INV + 4 * HIST_P
C_N = C_SEL + E

RING = 6
CH = 4096
EXPERT_CHUNKS = 6
FRONT_CHUNKS = 24
FRONT_SLOT = (0, 1, 2, 3) + (4, 5, 0, 1, 4, 5, 0, 1) + (4, 5, 0, 2) + (1, 3, 0, 1) + (2, 3, 4, 5)
HIGH_SLOT = (2, 3)

FRONT = (
    ["c_T", "chan_T"] + ["ada0", "mod_T"] + [f"x_T{k}" for k in range(KC)] + ["conv_hist_T", "pool_hist_T"]
    + [f"proj{m}" for m in (4, 5, 6, 7, 8, 9, 10, 11, 0, 1, 2, 3, 12, 13, 14, 15)]
    + [f"proj{m}" for m in range(16, 32)]
    + [f"pool{g}" for g in range(4)]
    + ["state_cp", "state_cs", "state_pp", "state_ps"] + ["ada1", "ada2"]
    + [f"out_a{m}" for m in range(8)] + [f"out_b{m}" for m in range(8)]
    + ["o00", "o01", "o10", "o11", "v_T00", "v_T01", "o2", "logits0", "v_T10", "v_T11", "logits1", "v_T20", "v_T21",
       "logits2", "rank", "counts", "bounds", "table", "gate_T"]
)
B_UP, B_X, B_DOWN, B_T, B_XT, B_C = (0, 1), 2, 3, 4, 5, (6, 7)
COMBINE_BANKS = (6, 7, 6, 7, 6)
PER_ROUND = [1, 1, 1, 1, 2, 1, 3, 2]


def front_place(name):
    n = FRONT.index(name)
    return n % 8, n // 8


def front_uses(bank):
    return len([n for n in range(len(FRONT)) if n % 8 == bank])


def program(nc, a, o):
    ctx = ExitStack()
    with ctx:
        def sb(name, shape, dt=F32):
            return ctx.enter_context(nc.sbuf_tensor(name, shape, dt))

        def sem(name):
            return ctx.enter_context(nc.semaphore(name))

        start = -(-nc.sbuf_base // 32) * 32
        ring = sb("ring", [P, RING, CH])
        front = sb("front", [P, 18720])
        hx = sb("hx", [P, 3, D])
        tail_rows = sb("tail_rows", [P, 4 * D])
        const = sb("const", [P, C_N])
        small = sb("small", [P, 700])
        table = sb("table", [1, 192], I32)
        top_index = sb("top_index", [P, 3, 8], U32)
        mod_rows = nc.dram_tensor("mod_rows", [NC_ROWS, 6 * D], F32)
        bank = [ctx.enter_context(nc.psum_tensor(f"bank{b}", [P, 512], F32)) for b in range(8)]

        def region(t, at, *shape):
            n = int(np.prod(shape))
            v = t[:, at:at + n]
            if len(shape) == 2:
                return v.rearrange("p (a b) -> p a b", a=shape[0])
            if len(shape) == 3:
                return v.rearrange("p (a b c) -> p a b c", a=shape[0], b=shape[1])
            return v

        ident = const[:, C_ID:C_ID + P]
        tri = const[:, C_TRI:C_TRI + P]
        ones = const[:, C_ONE:C_ONE + P]
        tri_incl = const[:, C_TRI1:C_TRI1 + E]
        iota = const[:, C_IOTA:C_IOTA + NT]
        sel3 = const[:, C_SEL:C_SEL + E]
        inv_count = region(const, C_INV, 4, HIST_P)

        u_T = region(front, 0, KC, NT)
        ring_parts = nc.alloc_sbuf_tensor_at("ring_parts", [P, RING, CH], F32R, offset=start)
        u_low = nc.alloc_sbuf_tensor_at("u_low", [P, KC, NT], F32R, offset=start + 4 * RING * CH)
        u_high = nc.alloc_sbuf_tensor_at("u_high", [P, KC, NT], F32R, offset=start + 4 * (RING * CH + 18720))
        b_T = region(front, 2560, 4, NT)
        c_T = region(front, 3840, 4, NT)
        z_p = region(front, 5120, 4, HIST_C + NP_TOK)
        z_s = region(front, 6152, 4, NSEQ, HIST_C + TSEQ)
        pool_p = region(front, 6472, 4, HIST_P + NP_TOK)
        pool_s = region(front, 7556, 4, NSEQ, HIST_P + TSEQ)
        diff_T = region(front, 8292, 4, NT)
        y_in_T = region(front, 9572, 4, NT)
        yg_T = region(front, 10852, 4, NT)
        ga_T = region(front, 12132, KC, NT)
        gb_T = region(front, 14692, KC, NT)
        sum_p = region(front, 17252, 2, HIST_P + NP_TOK)
        sum_s = region(front, 17800, 2, NSEQ, HIST_P + TSEQ)
        keep_s = region(front, 18168, 4, NSEQ, HIST_C)
        keep_ps = region(front, 18232, 4, NSEQ, HIST_P)
        c_rows = region(front, 12132, D)
        chan_rows = region(front, 13156, P)
        conv_hist = region(front, 10852, DC)
        pool_hist = region(front, 11364, DC)
        mod = region(tail_rows, 0, 3, 512)
        b_ada_rows = region(tail_rows, 1536, 3, 512)
        sg_c = region(small, 0, KC, NC_ROWS)
        sc_T = region(small, 72, KC, NC_ROWS)
        chan = region(small, 144, 16)
        state_rows = region(front, 0, 4, DC)
        V = region(front, 0, 3, D)
        b_up_rows = region(front, 3072, 2 * D)
        norm1_rows = region(front, 3072, 2, D)
        b_up_parts = region(front, 5120, D).bitcast(BF16)
        v_T = region(front, 8292, KC, NT)
        S = region(front, 6472, 3, SLOTS)
        S_gate = region(front, 6664, 3, P)
        x_rows = region(front, 7048, 512)
        up_sel = region(front, 7560, SLOTS // 2).bitcast(BF16)
        glu = region(front, 8292, 2, 256)
        lin = region(front, 8804, 2, 256)
        sig = region(front, 9316, 2, 256)
        act_rows = region(front, 9828, 512)
        act_T = region(front, 10340, 4, P)
        x_T = region(front, 10852, 4, P)
        P_gate = region(front, 11364, NT)
        O_rows = region(front, 11684, 2, 512)
        Y = region(front, 14692, 5, 512)
        y2_rows = region(front, 12708, 512)
        Y_2 = region(front, 13220, 512)
        w_pool = region(small, 160, 4, P)
        w_router = region(small, 160, KC, E)
        b_router = region(small, 672 - 256, E)
        mod_T = region(front, 17252 - 0, 4, P)
        stats = region(front, 17252, 12)
        aggr = region(front, 17264, 2)
        rstd = region(front, 17266, 1)
        ln_rows = region(front, 10852, D)
        rstd2 = region(front, 17267, 1)
        shift = region(front, 17268, 1)
        L = region(front, 17272, 3, E)
        top = region(front, 17368, 3, 8)
        top_f = region(front, 17392, 3, 8)
        mask = region(front, 17416, 3, E)
        eq = region(front, 17512, 3, E)
        gate = region(front, 17608, 3, E)
        gsum = region(front, 17704, 3)
        rank = region(front, 17707, 3, E)
        count = region(front, 17803, 1)
        rounds = region(front, 17804, 1)
        bound = region(front, 17805, 1)
        passed = region(front, 17806, NROUND)
        base_f = region(front, 17870, NROUND)

        bank_full = [sem(f"bank_full{b}") for b in range(8)]
        bank_free = [sem(f"bank_free{b}") for b in range(8)]
        chunk_landed = [sem(f"chunk_landed{s}") for s in range(RING)]
        chunk_used = [sem(f"chunk_used{s}") for s in range(RING)]
        const_landed = sem("const_landed")
        rows_landed = sem("rows_landed")
        x_landed = sem("x_landed")
        hist_landed = sem("hist_landed")
        bada_landed = sem("bada_landed")
        pool_w_landed = sem("pool_w_landed")
        router_landed = sem("router_landed")
        norm1_landed = sem("norm1_landed")
        tail_landed = sem("tail_landed")
        bias_landed = sem("bias_landed")
        mod_stored = sem("mod_stored")
        out_stored = sem("out_stored")
        dve_step = sem("dve_step")
        tail_step = sem("tail_step")
        c_sig_ready = sem("c_sig_ready")
        diff_ready = sem("diff_ready")
        conv_ready = sem("conv_ready")
        v_ready = sem("v_ready")
        keep_ready = sem("keep_ready")
        logit_ready = sem("logit_ready")
        var_ready = sem("var_ready")
        w_high_ready = sem("w_high_ready")
        w_low_ready = sem("w_low_ready")
        u_high_ready = sem("u_high_ready")
        u_low_ready = sem("u_low_ready")
        sqrt_ready = sem("sqrt_ready")
        rstd_ready = sem("rstd_ready")
        row_normed = sem("row_normed")
        o2_moved = sem("o2_moved")
        norm1_again = sem("norm1_again")
        h_step = sem("h_step")
        h_ready = sem("h_ready")
        exp_ready = sem("exp_ready")
        mask_ready = sem("mask_ready")
        rounds_ready = sem("rounds_ready")
        passed_ready = sem("passed_ready")
        table_ready = sem("table_ready")
        parts_step = sem("parts_step")
        b_up_ready = sem("b_up_ready")
        b_down_landed = sem("b_down_landed")
        O_cleared = sem("O_cleared")
        softmax_ready = sem("softmax_ready")
        sel_ready = sem("sel_ready")
        S_ready = sem("S_ready")
        gate_ready = sem("gate_ready")
        x_rows_ready = sem("x_rows_ready")
        xT_ready = sem("xT_ready")
        glu_ready = sem("glu_ready")
        sig_ready = sem("sig_ready")
        act_ready = sem("act_ready")
        actT_ready = sem("actT_ready")
        Pg_ready = sem("Pg_ready")
        O_ready = sem("O_ready")
        y_ready = sem("y_ready")

        block = ctx.enter_context(nc.Block())

        def front_slot(n):
            return FRONT_SLOT[n]

        def in_slot(n):
            return [m for m in range(n + 1) if front_slot(m) == front_slot(n)]

        def expert_slot(c):
            return (c + 2) % RING

        def landed_before(s):
            return FRONT_SLOT.count(s)

        def last_result(n):
            if n in (3, 15, 19):
                return f"ada{(3, 15, 19).index(n)}"
            if 4 <= n < 12:
                return f"proj{4 * IN_ORDER[n - 4] + 3}"
            return {20: "out_a7", 21: "out_b7", 23: "o2"}.get(n)

        def used_before(s):
            return len([n for n in range(FRONT_CHUNKS) if front_slot(n) == s and last_result(n) is None])

        def wait_chunk_read(eng, n):
            if last_result(n) is None:
                eng.wait_ge(chunk_used[front_slot(n)], len([m for m in in_slot(n) if last_result(m) is None]))
            else:
                wait_full(eng, last_result(n))

        IN_ORDER = (1, 2, 0, 3, 4, 5, 6, 7)
        ADA_CHUNK = [0, 12, 16]
        IN_CHUNK, OUTA_CHUNK, OUTB_CHUNK, O_CHUNK = 4, 20, 21, 22

        LAST_PROJ = f"proj{4 * IN_ORDER[7] + 3}"

        def wait_full(eng, name):
            b, n = front_place(name)
            eng.wait_ge(bank_full[b], n + 1)
            return bank[b]

        def wait_read(eng, name):
            b, n = front_place(name)
            eng.wait_ge(bank_free[b], n + 1)

        @block.sync
        def _(sp):
            w_ada = a["w_ada"][0].rearrange("(k p) n -> p k n", p=P)
            w_in = a["w_in"][0].rearrange("(k p) n -> p k n", p=P)

            def front_chunk(n, src, shape):
                s = front_slot(n)
                if s in HIGH_SLOT and n > 11:
                    wait_chunk_read(sp, 10 + HIGH_SLOT.index(s))
                if len(in_slot(n)) > 1:
                    wait_chunk_read(sp, in_slot(n)[-2])
                dst = ring[:, s, :].rearrange("p (a b) -> p a b", a=shape[0])
                sp.dma_start(dst, src).then_inc(chunk_landed[s], 16)

            sp.dma_start(const[:, :], a["const"]).then_inc(const_landed, 16)
            sp.dma_start(c_rows[0:1, :], a["c_prompt"]).then_inc(rows_landed, 16)
            sp.dma_start(c_rows[1:NC_ROWS, :], a["c_sample"]).then_inc(rows_landed, 16)
            sp.dma_start(chan_rows[0:12, :], a["conv_w"][0].rearrange("j (b i) -> (j b) i", i=P)).then_inc(rows_landed, 16)
            sp.dma_start(chan_rows[12:16, :], a["ls_pool"][0].rearrange("(b i) -> b i", i=P)).then_inc(rows_landed, 16)
            for i in range(4):
                front_chunk(ADA_CHUNK[0] + i, w_ada[:, 2 * i:2 * i + 2, 0:2048], (2, 2048))
                if i == 0:
                    for q in range(4):
                        src = a["b_ada"][0].rearrange("(n q m) -> n q m", n=3, q=4)[:, q, :]
                        sp.dma_start(b_ada_rows[32 * q:32 * q + NC_ROWS, :, :], src.partition_broadcast(NC_ROWS)).then_inc(bada_landed, 16)
                if i == 1:
                    sp.dma_start(hx[:, 0:2, :], a["x_prompt"][0].rearrange("(t p) d -> p t d", p=P)).then_inc(x_landed, 16)
                    sp.dma_start(hx[0:NS_TOK, 2, :], a["x_sample"].rearrange("s t d -> (s t) d")).then_inc(x_landed, 16)
            for i in range(8):
                m = IN_ORDER[i]
                front_chunk(IN_CHUNK + i, w_in[:, :, m * 512:(m + 1) * 512], (8, 512))
                if i == 1:
                    sp.dma_start(conv_hist[0:NSEQ * HIST_C, :], a["state_conv"][0].rearrange("s t d -> (s t) d")).then_inc(hist_landed, 16)
                    sp.dma_start(pool_hist[0:NSEQ * HIST_P, :], a["state_pool"][0].rearrange("s t d -> (s t) d")).then_inc(hist_landed, 16)
            for third in (1, 2):
                for i in range(4):
                    front_chunk(ADA_CHUNK[third] + i,
                                w_ada[:, 2 * i:2 * i + 2, third * 2048:(third + 1) * 2048], (2, 2048))
                    if third == 2 and i == 2:
                        wait_full(sp, LAST_PROJ)
                        sp.dma_start(hx[:, 0:2, :], a["x_prompt"][0].rearrange("(t p) d -> p t d", p=P)).then_inc(x_landed, 16)
                        sp.dma_start(hx[0:NS_TOK, 2, :], a["x_sample"].rearrange("s t d -> (s t) d")).then_inc(x_landed, 16)
            front_chunk(OUTA_CHUNK, a["w_out_a"][0].rearrange("(k p) n -> p k n", p=P), (4, D))
            front_chunk(OUTB_CHUNK, a["w_out_b"][0].rearrange("(k p) n -> p k n", p=P), (4, D))
            for i in range(2):
                front_chunk(O_CHUNK + i, a["w_o"][0, i * 512:(i + 1) * 512, :].rearrange("(k p) n -> p k n", p=P),
                            (4, D))
            wait_chunk_read(sp, 18)
            wait_chunk_read(sp, 19)
            sp.wait_ge(mod_stored, 16 * 12)
            sp.dma_start(ring[:, 0, 0:3 * D], mod_rows[0, 2 * D:5 * D].partition_broadcast(P)).then_inc(norm1_landed, 16)
            sp.dma_start(ring[:, 0, 3 * D:], a["ln1_g"][0].partition_broadcast(P)).then_inc(norm1_landed, 16)
            for s in range(NSEQ):
                sp.dma_start(ring[TSEQ * s:TSEQ * (s + 1), 1, 0:3 * D],
                             mod_rows[1 + s, 2 * D:5 * D].partition_broadcast(TSEQ)).then_inc(norm1_landed, 16)
            sp.dma_start(ring[:, 1, 3 * D:], a["ln1_b"][0].partition_broadcast(P)).then_inc(norm1_landed, 16)

            def expert_chunk(c, e):
                s = expert_slot(c)
                if c < 4:
                    j, half = divmod(c, 2)
                    for g in range(2):
                        src = a["w_up"][0][:, half * 512:(half + 1) * 512, g * D + j * 512:g * D + (j + 1) * 512]
                        sp.dma_start(ring[:, s, g * 2048:(g + 1) * 2048].rearrange("p (k m) -> p k m", k=4),
                                     src.rearrange("e (k p) m -> p e k m", p=P)[:, e]).then_inc(chunk_landed[s], 16)
                else:
                    src = a["w_down"][0][:, (c - 4) * 512:(c - 3) * 512, :].rearrange("e (k p) m -> p e k m", p=P)
                    sp.dma_start(ring[:, s, :].rearrange("p (k m) -> p k m", k=4), src[:, e]).then_inc(chunk_landed[s], 16)

            for c in range(EXPERT_CHUNKS):
                if expert_slot(c) < 2:
                    sp.wait_ge(v_ready, 3)
                else:
                    wait_chunk_read(sp, 18 + expert_slot(c))
                expert_chunk(c, 0)
            sp.wait_ge(table_ready, 1)
            ends_with = {1: B_UP[0], 3: B_UP[1], 5: B_DOWN}
            with sp.Fori(1, E) as e:
                rounds_done = sp.value_load(table[0:1, bass.ds(e + 127, 1)], min_val=1, max_val=52)
                for c in range(EXPERT_CHUNKS):
                    if c in ends_with:
                        b = ends_with[c]
                        sp.wait_ge(bank_full[b], rounds_done + front_uses(b))
                    else:
                        s = expert_slot(c)
                        sp.wait_ge(chunk_used[s], rounds_done + used_before(s))
                    expert_chunk(c, e)

        @block.gpsimd
        def _(pool):
            pool.dma_start(w_pool, a["w_pool"][0].rearrange("g c d -> c g d")).then_inc(pool_w_landed, 16)
            for i in range(8):
                slot = front_slot(IN_CHUNK + i)
                for q in range(4):
                    pool.wait_ge(w_high_ready, 4 * i + q + 1)
                    part = slice(q * 1024, (q + 1) * 1024)
                    pool.tensor_tensor(ring_parts[:, slot, part], ring[:, slot, part],
                                       ring_parts[:, HIGH_SLOT[i % 2], part].bitcast(F32), ALU.subtract).then_inc(w_low_ready, 1)
            for name in ("state_cp", "state_cs", "state_pp", "state_ps"):
                wait_read(pool, name)
            rows = ((o["conv_p"][0, 0], 2, 0), (o["conv_s"][0].rearrange("s t d -> (s t) d"), 16, 1),
                    (o["pool_p"][0, 0], 15, 2), (o["pool_s"][0].rearrange("s t d -> (s t) d"), 120, 3))
            for dst, n, i in rows:
                pool.dma_start(dst, state_rows[0:n, i, :]).then_inc(out_stored, 16)
            for n in range(3):
                wait_read(pool, f"ada{n}")
                for q in range(4):
                    pool.dma_start(mod_rows[:, n * 2048 + q * 512:n * 2048 + (q + 1) * 512],
                                   mod[32 * q:32 * q + NC_ROWS, n, :]).then_inc(mod_stored, 16)
            wait_full(pool, "pool3")
            pool.dma_start(w_router, a["w_router"][0].rearrange("(k p) e -> p k e", p=P)).then_inc(router_landed, 16)
            pool.dma_start(b_router, a["b_router"][0].partition_broadcast(P)).then_inc(router_landed, 16)
            pool.wait_ge(mod_stored, 16 * 12)
            pool.dma_start(tail_rows[:, 0:D], mod_rows[0, 5 * D:].partition_broadcast(P)).then_inc(tail_landed, 16)
            for s in range(NSEQ):
                pool.dma_start(tail_rows[TSEQ * s:TSEQ * (s + 1), D:2 * D],
                               mod_rows[1 + s, 5 * D:].partition_broadcast(TSEQ)).then_inc(tail_landed, 16)
            pool.dma_start(tail_rows[:, 2 * D:3 * D], a["ln2_g"][0].partition_broadcast(P)).then_inc(tail_landed, 16)
            pool.dma_start(tail_rows[:, 3 * D:], a["ln2_b"][0].partition_broadcast(P)).then_inc(tail_landed, 16)
            wait_full(pool, "state_ps")
            pool.wait_ge(conv_ready, 4)
            for q in range(3):
                pool.dma_start(b_up_rows[32 * q:32 * q + E, :], a["b_up"][0]).then_inc(bias_landed, 16)
            done = [0]

            def part(ins):
                done[0] += 1
                ins.then_inc(parts_step, 1)
                pool.wait_ge(parts_step, done[0])

            part(pool.memset(b_up_parts, 0.0))
            pool.wait_ge(bias_landed, 48)
            for q in range(3):
                rows, parts = b_up_rows[32 * q:32 * q + E, :], b_up_parts[32 * q:32 * q + E, :]
                for i in range(q):
                    part(pool.tensor_copy(parts, rows))
                    part(pool.tensor_tensor(rows, rows, parts, ALU.subtract))
                part(pool.tensor_copy(parts, rows))
            pool.memset(b_up_rows[0:1, 0:1], 0.0).then_inc(b_up_ready, 1)
            pool.wait_ge(O_cleared, 1)
            pool.dma_start(O_rows[0:E, :, :], a["b_down"][0].rearrange("e (h m) -> e h m", h=2)).then_inc(b_down_landed, 16)
            pool.wait_ge(b_up_ready, 1)
            pool.dma_start(norm1_rows[:, 0, :], a["ln1_g"][0].partition_broadcast(P)).then_inc(norm1_again, 16)
            pool.dma_start(norm1_rows[:, 1, :], a["ln1_b"][0].partition_broadcast(P)).then_inc(norm1_again, 16)
            pool.wait_ge(norm1_again, 32)
            for t in range(3):
                r = ROWS[t]
                row = hx[0:r, t, :]
                pool.wait_ge(v_ready, t + 1)
                pool.tensor_tensor(row, row, norm1_rows[0:r, 0, :], ALU.mult).then_inc(h_step, 1)
                pool.wait_ge(h_step, 2 * t + 1)
                pool.tensor_tensor(row, row, norm1_rows[0:r, 1, :], ALU.add).then_inc(h_step, 1)
                pool.wait_ge(h_step, 2 * t + 2)
                pool.tensor_scalar(row, row, ALPHA, 1.0, ALU.mult, ALU.mult).then_inc(h_ready, 1)
            outs = (o["y_p"][0, 0:P], o["y_p"][0, P:2 * P], o["y_s"].rearrange("s t d -> (s t) d"))
            for t in range(2):
                row = V[:, t, :]
                pool.wait_ge(row_normed, 4 + t)
                pool.tensor_tensor(row, row, tail_rows[:, 2 * D:3 * D], ALU.mult).then_inc(h_step, 1)
                pool.wait_ge(h_step, 7 + 2 * t)
                pool.tensor_tensor(row, row, tail_rows[:, 3 * D:], ALU.add).then_inc(h_step, 1)
                pool.wait_ge(h_step, 8 + 2 * t)
                pool.dma_start(outs[t], row).then_inc(out_stored, 16)
            pool.wait_ge(y_ready, 1)
            pool.dma_start(outs[2], V[0:NS_TOK, 2, :]).then_inc(out_stored, 16)
            pool.wait_ge(out_stored, 16 * 7)

        @block.tensor
        def _(pe):
            mm = nc.tensor.matmul

            def take(name):
                b, n = front_place(name)
                if n:
                    pe.wait_ge(bank_free[b], n)
                return bank[b]

            def done(name, ins):
                ins.then_inc(bank_full[front_place(name)[0]], 1)

            def chunk(n):
                s = front_slot(n)
                pe.wait_ge(chunk_landed[s], 16 * len(in_slot(n)))
                return ring[:, s, :]

            pe.wait_ge(const_landed, 16)
            pe.wait_ge(rows_landed, 64)
            ps = take("c_T")
            for k in range(KC):
                last = nc.tensor.transpose(ps[:, k * NC_ROWS:(k + 1) * NC_ROWS], c_rows[0:NC_ROWS, k * P:(k + 1) * P],
                                           ident[0:NC_ROWS, 0:NC_ROWS])
            done("c_T", last)
            ps = take("chan_T")
            done("chan_T", nc.tensor.transpose(ps[:, 0:16], chan_rows[0:16, :], ident[0:16, 0:16]))

            def ada(third):
                ps = take(f"ada{third}")
                for i in range(4):
                    w = chunk(ADA_CHUNK[third] + i).rearrange("p (a b) -> p a b", a=2)
                    for kk in range(2):
                        k = 2 * i + kk
                        for q in range(4):
                            last = mm(ps[32 * q:32 * q + NC_ROWS, :], sc_T[:, k, :], w[:, kk, q * 512:(q + 1) * 512],
                                      start=k == 0, stop=k == KC - 1)
                    if i < 3:
                        last.then_inc(chunk_used[front_slot(ADA_CHUNK[third] + i)], 1)
                done(f"ada{third}", last)

            wait_read(pe, "c_T")
            ada(0)
            wait_read(pe, "ada0")
            ps = take("mod_T")
            for blk in range(4):
                last = nc.tensor.transpose(ps[:, blk * P:(blk + 1) * P], mod[:, 0, blk * P:(blk + 1) * P], ident)
            done("mod_T", last)
            pe.wait_ge(x_landed, 32)
            for k in range(KC):
                ps = take(f"x_T{k}")
                for t in range(3):
                    r = ROWS[t]
                    last = nc.tensor.transpose(ps[:, t * P:t * P + r], hx[0:r, t, k * P:(k + 1) * P], ident[0:r, 0:r])
                done(f"x_T{k}", last)
            pe.wait_ge(hist_landed, 32)
            for name, src, r in (("conv_hist_T", conv_hist, 16), ("pool_hist_T", pool_hist, 120)):
                ps = take(name)
                for blk in range(4):
                    last = nc.tensor.transpose(ps[:, blk * r:(blk + 1) * r], src[0:r, blk * P:(blk + 1) * P], ident[0:r, 0:r])
                done(name, last)

            def proj(i, m4):
                low = ring_parts[:, front_slot(IN_CHUNK + i), :].rearrange("p (k m) -> p k m", k=KC)
                high = ring_parts[:, HIGH_SLOT[i % 2], :].rearrange("p (k m) -> p k m", k=KC)
                for j in range(4):
                    name = f"proj{4 * m4 + j}"
                    ps = take(name)
                    for part, w, u in (("high high", high, u_high), ("high low", high, u_low), ("low high", low, u_high)):
                        for k in range(KC):
                            if j == 0 and k % 2 == 0 and part == "high high":
                                pe.wait_ge(w_high_ready, 4 * i + k // 2 + 1)
                            if j == 0 and k % 2 == 0 and part == "low high":
                                pe.wait_ge(w_low_ready, 4 * i + k // 2 + 1)
                            if i == 0 and j == 0 and part == "high high":
                                pe.wait_ge(u_high_ready, k + 1)
                            if i == 0 and j == 0 and part == "high low":
                                pe.wait_ge(u_low_ready, k + 1)
                            last = mm(ps[:, 0:NT], w[:, k, j * P:(j + 1) * P], u[:, k, :],
                                      start=part == "high high" and k == 0, stop=part == "low high" and k == KC - 1)
                    done(name, last)

            for i in range(8):
                proj(i, IN_ORDER[i])
            pe.wait_ge(pool_w_landed, 16)
            for g in range(4):
                pe.wait_ge(diff_ready, g + 1)
                ps = take(f"pool{g}")
                done(f"pool{g}", mm(ps[:, 0:NT], w_pool[:, g, :], diff_T[:, g, :], start=True, stop=True))

            pe.wait_ge(keep_ready, 2)
            pieces = (("state_cp", 2, lambda b: z_p[:, b, NP_TOK:]),
                      ("state_cs", 16, lambda b: keep_s[:, b, :, :].rearrange("p s t -> p (s t)")),
                      ("state_pp", 15, lambda b: pool_p[:, b, NP_TOK:]),
                      ("state_ps", 120, lambda b: keep_ps[:, b, :, :].rearrange("p s t -> p (s t)")))
            for name, r, piece in pieces:
                ps = take(name)
                for b in range(4):
                    last = nc.tensor.transpose(ps[0:r, b * P:(b + 1) * P], piece(b), ident)
                done(name, last)
            ada(1)
            ada(2)
            pe.wait_ge(conv_ready, 4)
            w = chunk(OUTA_CHUNK).rearrange("p (k m) -> p k m", k=4)
            for m in range(8):
                ps = take(f"out_a{m}")
                for k in range(4):
                    last = mm(ps[:, 0:NT], w[:, k, m * P:(m + 1) * P], y_in_T[:, k, :], start=k == 0, stop=k == 3)
                done(f"out_a{m}", last)
            for g in range(4):
                wait_read(pe, f"pool{g}")
            w = chunk(OUTB_CHUNK).rearrange("p (k m) -> p k m", k=4)
            for m in range(8):
                ps = take(f"out_b{m}")
                for k in range(4):
                    last = mm(ps[:, 0:NT], w[:, k, m * P:(m + 1) * P], yg_T[:, k, :], start=k == 0, stop=k == 3)
                done(f"out_b{m}", last)
            wo = [chunk(O_CHUNK + i).rearrange("p (k m) -> p k m", k=4) for i in range(2)]
            for t in range(2):
                for h in range(2):
                    ps = take(f"o{t}{h}")
                    for k in range(KC):
                        if t == 0 and h == 0:
                            wait_read(pe, f"out_b{k}")
                        last = mm(ps[:, :], ga_T[:, k, t * P:(t + 1) * P], wo[k // 4][:, k % 4, h * 512:(h + 1) * 512],
                                  start=k == 0, stop=k == KC - 1)
                    done(f"o{t}{h}", last)

            def v_transposes(t):
                pe.wait_ge(v_ready, t + 1)
                r = ROWS[t]
                for half in range(2):
                    ps = take(f"v_T{t}{half}")
                    for i in range(4):
                        k = 4 * half + i
                        last = nc.tensor.transpose(ps[:, i * P:i * P + r], V[0:r, t, k * P:(k + 1) * P], ident[0:r, 0:r])
                    done(f"v_T{t}{half}", last)

            def logits(t):
                ps = take(f"logits{t}")
                for k in range(KC):
                    if k % 4 == 0:
                        wait_read(pe, f"v_T{t}{k // 4}")
                    last = mm(ps[0:ROWS[t], 0:E], v_T[:, k, t * P:t * P + ROWS[t]], w_router[:, k, :],
                              start=k == 0, stop=k == KC - 1)
                done(f"logits{t}", last)

            v_transposes(0)
            ps = take("o2")
            for k in range(KC):
                for h in range(2):
                    last = mm(ps[64 * h:64 * h + 64, :], ga_T[:, k, 2 * P:NT], wo[k // 4][:, k % 4, h * 512:(h + 1) * 512],
                              start=k == 0, stop=k == KC - 1)
                if k == 3:
                    last.then_inc(chunk_used[front_slot(O_CHUNK)], 1)
            done("o2", last)
            pe.wait_ge(router_landed, 32)
            logits(0)
            for t in (1, 2):
                v_transposes(t)
                logits(t)
            pe.wait_ge(mask_ready, 1)
            ps = take("rank")
            for t in range(3):
                for i in range(t + 1):
                    lhs = tri if i == t else ones
                    last = mm(ps[0:ROWS[t], t * E:(t + 1) * E], lhs[0:ROWS[i], 0:ROWS[t]], mask[0:ROWS[i], i, :],
                              start=i == 0, stop=i == t)
            done("rank", last)
            ps = take("counts")
            for t in range(3):
                last = mm(ps[0:E, 0:1], mask[0:ROWS[t], t, :], ones[0:ROWS[t], 0:1], start=t == 0, stop=t == 2)
            done("counts", last)
            pe.wait_ge(rounds_ready, 1)
            ps = take("bounds")
            done("bounds", mm(ps[0:E, 0:1], tri_incl[0:E, :], rounds[0:E, :], start=True, stop=True))
            pe.wait_ge(passed_ready, 1)
            ps = take("table")
            mm(ps[0:1, 0:NROUND], ones[0:E, 0:1], passed[0:E, :], start=True, stop=True)
            mm(ps[0:1, NROUND:2 * NROUND], rounds[0:E, :], passed[0:E, :], start=True, stop=True)
            done("table", mm(ps[0:1, 2 * NROUND:2 * NROUND + E], rounds[0:E, :], tri_incl[0:E, :], start=True, stop=True))

            pe.wait_ge(softmax_ready, 1)
            ps = take("gate_T")
            for t in range(3):
                r = ROWS[t]
                last = nc.tensor.transpose(ps[0:E, t * P:t * P + r], gate[0:r, t, :], ident[0:r, 0:r])
            done("gate_T", last)

            def gather(n, x_rows_read=None):
                pe.wait_ge(S_ready, n + 1)
                if x_rows_read is not None:
                    pe.wait_ge(x_rows_ready, x_rows_read)
                for t in range(3):
                    for h in range(2):
                        last = mm(bank[B_X][64 * h:64 * h + 64, :], S[0:ROWS[t], t, :], V[0:ROWS[t], t, h * 512:(h + 1) * 512],
                                  start=t == 0, stop=t == 2)
                last.then_inc(bank_full[B_X], 1)

            def x_transposes(n, xT_read=None):
                pe.wait_ge(x_rows_ready, n + 1)
                if xT_read is not None:
                    pe.wait_ge(xT_ready, xT_read)
                for q in range(4):
                    last = nc.tensor.transpose(bank[B_XT][:, q * P:(q + 1) * P], x_rows[:, q * P:(q + 1) * P], ident)
                last.then_inc(bank_full[B_XT], 1)

            def combine(n, pieces):
                for i in pieces:
                    b = COMBINE_BANKS[i]
                    if i == 0:
                        pe.wait_ge(O_ready, 2 * n + 2)
                        pe.wait_ge(Pg_ready, n + 1)
                    pe.wait_ge(bank_free[b], front_uses(b) + PER_ROUND[b] * n + COMBINE_BANKS[:i].count(b))
                    if i < 4:
                        t, h = divmod(i, 2)
                        last = mm(bank[b][:, :], P_gate[:, t * P:(t + 1) * P], O_rows[:, h, :], start=True, stop=True)
                    else:
                        for h in range(2):
                            last = mm(bank[b][64 * h:64 * h + 64, :], P_gate[:, 2 * P:NT], O_rows[:, h, :],
                                      start=True, stop=True)
                    last.then_inc(bank_full[b], 1)

            pe.wait_ge(table_ready, 1)
            G = pe.value_load(table[0:1, 159:160], min_val=1, max_val=52)
            gather(0)
            x_transposes(0)
            pe.wait_ge(b_up_ready, 1)
            with pe.Fori(0, G) as g:
                e = pe.value_load(table[0:1, bass.ds(g, 1)], min_val=0, max_val=E - 1)
                for j in range(2):
                    b = B_UP[j]
                    pe.wait_ge(bank_free[b], g + front_uses(b))
                    if j == 0:
                        pe.wait_ge(sel_ready, g + 1)
                    for h in range(2):
                        at = j * 512 + h * 256
                        mm(bank[b][64 * h:64 * h + 64, :], up_sel,
                           b_up_parts.rearrange("p (g m) -> p g m", g=2)[:, :, at:at + 256], start=True, stop=False)
                    if j == 0:
                        pe.wait_ge(xT_ready, g + 1)
                    for k in range(KC):
                        s = expert_slot(2 * j + k // 4)
                        if k % 4 == 0:
                            pe.wait_ge(chunk_landed[s], e * 32 + 16 * landed_before(s) + 32)
                        w = ring[:, s, :].rearrange("p (g k m) -> p g k m", g=2, k=4)[:, :, k % 4, :]
                        for h in range(2):
                            last = mm(bank[b][64 * h:64 * h + 64, :], x_T[:, k % 4, 64 * (k // 4):64 * (k // 4) + 64],
                                      w[:, :, h * 256:(h + 1) * 256], start=False, stop=k == KC - 1)
                        if k == 3:
                            last.then_inc(chunk_used[s], 1)
                    last.then_inc(bank_full[b], 1)
                gather(g + 1, x_rows_read=g + 1)
                combine(g, (0, 1, 2))
                pe.wait_ge(act_ready, 2 * g + 2)
                pe.wait_ge(Pg_ready, g + 1)
                for q in range(4):
                    last = nc.tensor.transpose(bank[B_T][:, q * P:(q + 1) * P], act_rows[:, q * P:(q + 1) * P], ident)
                last.then_inc(bank_full[B_T], 1)
                x_transposes(g + 1, xT_read=g + 1)
                combine(g, (3, 4))
                pe.wait_ge(gate_ready, g + 1)
                pe.wait_ge(actT_ready, g + 1)
                for t in range(3):
                    r = ROWS[t]
                    last = nc.tensor.transpose(bank[B_T][:, t * P:t * P + r], S_gate[0:r, t, :], ident[0:r, 0:r])
                last.then_inc(bank_full[B_T], 1)
                for k in range(KC):
                    s = expert_slot(4 + k // 4)
                    if k % 4 == 0:
                        pe.wait_ge(chunk_landed[s], e * 16 + 16 * landed_before(s) + 16)
                    q, hh = 2 * (k // 4) + k % 2, (k % 4) // 2
                    for h in range(2):
                        last = mm(bank[B_DOWN][64 * h:64 * h + 64, :], act_T[:, q, 64 * hh:64 * hh + 64],
                                  ring[:, s, (k % 4) * 1024 + h * 512:(k % 4) * 1024 + (h + 1) * 512], start=k == 0, stop=k == KC - 1)
                    if k == 3:
                        last.then_inc(chunk_used[s], 1)
                last.then_inc(bank_full[B_DOWN], 1)
            combine(G, range(5))

        @block.scalar
        def _(act):
            AF = nc.scalar.activation

            def free(name, ins):
                ins.then_inc(bank_free[front_place(name)[0]], 1)

            ps = wait_full(act, "c_T")
            AF(sg_c, ps[:, 0:KC * NC_ROWS].rearrange("p (k b) -> p k b", k=KC), ACT.Sigmoid).then_inc(c_sig_ready, 1)

            def split_high(i):
                n = IN_CHUNK + i
                s = front_slot(n)
                if i < 2:
                    wait_chunk_read(act, HIGH_SLOT[i])
                act.wait_ge(chunk_landed[s], 16 * len(in_slot(n)))
                for q in range(4):
                    part = slice(q * 1024, (q + 1) * 1024)
                    AF(ring_parts[:, HIGH_SLOT[i % 2], part], ring[:, s, part], ACT.Copy).then_inc(w_high_ready, 1)

            split_high(0)
            for k in range(KC):
                if k == 0:
                    wait_full(act, f"x_T{KC - 1}")
                wait_read(act, f"x_T{k}")
                AF(u_high[:, k, :], u_T[:, k, :], ACT.Copy).then_inc(u_high_ready, 1)
            split_high(1)
            for i, m4 in enumerate(IN_ORDER):
                for m in range(4 * m4, 4 * m4 + 4):
                    ps = wait_full(act, f"proj{m}")
                    if m4 == 0:
                        free(f"proj{m}", AF(b_T[:, m, :], ps[:, 0:NT], ACT.Copy))
                    elif m4 == 1:
                        free(f"proj{m}", AF(c_T[:, m - 4, :], ps[:, 0:NT], ACT.Copy))
                    elif m4 >= 4:
                        dst = ga_T if m < 24 else gb_T
                        free(f"proj{m}", AF(dst[:, (m - 16) % 8, :], ps[:, 0:NT], ACT.Sigmoid))
                if i + 2 < 8:
                    split_high(i + 2)
            for i, (name, r) in enumerate((("state_cp", 2), ("state_cs", 16), ("state_pp", 15), ("state_ps", 120))):
                ps = wait_full(act, name)
                free(name, AF(state_rows[0:r, i, :], ps[0:r, :], ACT.Copy))
            def root(n, row):
                r = ROWS[n % 3]
                if n:
                    act.wait_ge(row_normed, n)
                act.wait_ge(var_ready, n + 1)
                AF(rstd[0:r, :], aggr[0:r, 1:2], ACT.Sqrt).then_inc(sqrt_ready, 1)
                act.wait_ge(rstd_ready, n + 1)
                AF(row, row, ACT.Identity, bias=shift[0:r, :], scale=rstd[0:r, :]).then_inc(row_normed, 1)

            def vT_copy(t):
                r = ROWS[t]
                for half in range(2):
                    ps = wait_full(act, f"v_T{t}{half}")[:, :].rearrange("p (k t) -> p k t", k=4)
                    free(f"v_T{t}{half}", AF(v_T[:, 4 * half:4 * half + 4, t * P:t * P + r], ps[:, :, 0:r], ACT.Copy))

            root(0, hx[:, 0, :])
            root(1, hx[:, 1, :])
            vT_copy(0)
            ps = wait_full(act, "o2")
            act.wait_ge(row_normed, 2)
            AF(ln_rows[0:NS_TOK, 512:], ps[64:P, :], ACT.Copy).then_inc(o2_moved, 1)
            root(2, hx[0:NS_TOK, 2, :])
            vT_copy(1)
            vT_copy(2)
            act.wait_ge(logit_ready, 1)
            AF(gate[:, :, :], eq[:, :, :], ACT.Exp).then_inc(exp_ready, 1)

            def x_copy(n):
                act.wait_ge(bank_full[B_X], front_uses(B_X) + n + 1)
                AF(x_rows[:, :], bank[B_X][:, :], ACT.Copy).then_inc(x_rows_ready, 1)

            def xT_copy(n):
                act.wait_ge(bank_full[B_XT], front_uses(B_XT) + n + 1)
                AF(x_T[:, :, :], bank[B_XT][:, :].rearrange("p (q s) -> p q s", q=4), ACT.Copy).then_inc(xT_ready, 1)

            act.wait_ge(table_ready, 1)
            G = act.value_load(table[0:1, 159:160], min_val=1, max_val=52)
            x_copy(0)
            xT_copy(0)
            with act.Fori(0, G) as g:
                for j in range(2):
                    act.wait_ge(glu_ready, 2 * g + j + 1)
                    AF(sig[:, j, :], glu[:, j, :], ACT.Sigmoid, scale=SWISH).then_inc(sig_ready, 1)
                x_copy(g + 1)
                act.wait_ge(bank_full[B_T], front_uses(B_T) + 2 * g + 1)
                AF(act_T[:, :, :], bank[B_T][:, :].rearrange("p (q s) -> p q s", q=4), ACT.Copy).then_inc(actT_ready, 1)
                xT_copy(g + 1)
                act.wait_ge(bank_full[B_T], front_uses(B_T) + 2 * g + 2)
                AF(P_gate[0:SLOTS, :], bank[B_T][0:SLOTS, 0:NT], ACT.Copy).then_inc(Pg_ready, 1)
                act.wait_ge(bank_full[B_DOWN], g + front_uses(B_DOWN) + 1)
                for h in range(2):
                    AF(O_rows[0:SLOTS, h, :], bank[B_DOWN][64 * h:64 * h + 64, :], ACT.Copy).then_inc(O_ready, 1)
            root(3, V[:, 0, :])
            act.wait_ge(bank_full[COMBINE_BANKS[4]], front_uses(6) + 3 * (G + 1))
            AF(y2_rows[0:NS_TOK, :], bank[6][64:P, :], ACT.Copy).then_inc(o2_moved, 1)
            root(4, V[:, 1, :])
            root(5, V[0:NS_TOK, 2, :])

        @block.vector
        def _(dve):
            v = nc.vector
            steps = [0]
            origin = [0]
            step_sem = [dve_step]

            def step(ins):
                steps[0] += 1
                ins.then_inc(step_sem[0], 1)
                dve.wait_ge(step_sem[0], origin[0] + steps[0])

            def signal(ins, sem, value):
                ins.then_inc(sem, 1)
                dve.wait_ge(sem, value)

            def free(name, ins):
                b, n = front_place(name)
                signal(ins, bank_free[b], n + 1)

            TS, TT, STT = v.tensor_scalar, v.tensor_tensor, v.scalar_tensor_tensor
            step(v.memset(mod[:, 0, :], 0.0))
            step(v.memset(z_p[:, :, 0:HIST_C], 0.0))
            step(v.memset(pool_p[:, :, 0:HIST_P], 0.0))
            dve.wait_ge(c_sig_ready, 1)
            ps = wait_full(dve, "c_T")
            free("c_T", TT(sc_T, ps[:, 0:KC * NC_ROWS].rearrange("p (k b) -> p k b", k=KC), sg_c, ALU.mult))
            ps = wait_full(dve, "chan_T")
            free("chan_T", v.tensor_copy(chan, ps[:, 0:16]))
            dve.wait_ge(bada_landed, 64)

            def ada(third):
                ps = wait_full(dve, f"ada{third}")
                for q in range(4):
                    r = slice(32 * q, 32 * q + NC_ROWS)
                    ins = TT(mod[r, third, :], ps[r, :], b_ada_rows[r, third, :], ALU.add)
                    if q < 3:
                        step(ins)
                    else:
                        free(f"ada{third}", ins)

            ada(0)
            ps = wait_full(dve, "mod_T")[:, :].rearrange("p (b r) -> p b r", b=4)
            step(v.tensor_copy(mod_T[:, :, 0:64], ps[:, :, 0:64]))
            free("mod_T", TS(mod_T[:, :, 64:P], ps[:, :, 64:P], 1.0, None, ALU.add))
            for k in range(KC):
                ps = wait_full(dve, f"x_T{k}")
                q, blk = divmod(k, 4)
                sh, sc = mod_T[:, blk, 32 * q:32 * q + NC_ROWS], mod_T[:, blk, 32 * q + 64:32 * q + 64 + NC_ROWS]
                by_seq = lambda t: t.rearrange("p (s t) -> p s t", s=NSEQ)
                wide = lambda t: t[:, 1:NC_ROWS].unsqueeze(2).to_broadcast([P, NSEQ, TSEQ])
                step(TS(u_T[:, k, 0:NP_TOK], ps[:, 0:NP_TOK], sc[:, 0:1], sh[:, 0:1], ALU.mult, ALU.add))
                step(TT(by_seq(u_T[:, k, NP_TOK:]), by_seq(ps[:, NP_TOK:NT]), wide(sc), ALU.mult))
                free(f"x_T{k}", TT(by_seq(u_T[:, k, NP_TOK:]), by_seq(u_T[:, k, NP_TOK:]), wide(sh), ALU.add))
            for k in range(KC):
                dve.wait_ge(u_high_ready, k + 1)
                signal(TT(u_low[:, k, :], u_T[:, k, :], u_high[:, k, :].bitcast(F32), ALU.subtract), u_low_ready, k + 1)
            ps = wait_full(dve, "conv_hist_T")
            free("conv_hist_T", v.tensor_copy(z_s[:, :, :, 0:HIST_C], ps[:, 0:64].rearrange("p (b s t) -> p b s t", b=4, s=NSEQ)))
            ps = wait_full(dve, "pool_hist_T")
            free("pool_hist_T", v.tensor_copy(pool_s[:, :, :, 0:HIST_P], ps[:, 0:480].rearrange("p (b s t) -> p b s t", b=4, s=NSEQ)))
            for b in range(4):
                ps = wait_full(dve, f"proj{8 + b}")
                wait_read(dve, f"proj{4 + b}")
                step(TT(z_p[:, b, HIST_C:], ps[:, 0:NP_TOK], c_T[:, b, 0:NP_TOK], ALU.mult))
                free(f"proj{8 + b}", TT(z_s[:, b, :, HIST_C:], by_seq(ps[:, NP_TOK:NT]), by_seq(c_T[:, b, NP_TOK:]), ALU.mult))
            for b in range(4):
                ps = wait_full(dve, f"proj{12 + b}")
                step(v.tensor_copy(pool_p[:, b, HIST_P:], ps[:, 0:NP_TOK]))
                free(f"proj{12 + b}", v.tensor_copy(pool_s[:, b, :, HIST_P:], by_seq(ps[:, NP_TOK:NT])))
            signal(v.tensor_copy(keep_s, z_s[:, :, :, TSEQ:]), keep_ready, 1)
            signal(v.tensor_copy(keep_ps, pool_s[:, :, :, TSEQ:]), keep_ready, 2)
            for g, w in enumerate(WINDOWS):
                src_p, src_s = pool_p[:, g, :], pool_s[:, g, :, :]
                reach, n = 1, 0
                while reach < w:
                    dp, ds_ = sum_p[:, n % 2, :], sum_s[:, n % 2, :, :]
                    lo = 2 * reach - 1
                    step(TT(dp[:, lo:], src_p[:, lo:], src_p[:, lo - reach:HIST_P + NP_TOK - reach], ALU.add))
                    step(TT(ds_[:, :, lo:], src_s[:, :, lo:], src_s[:, :, lo - reach:HIST_P + TSEQ - reach], ALU.add))
                    src_p, src_s = dp, ds_
                    reach, n = 2 * reach, n + 1
                step(STT(diff_T[:, g, 0:NP_TOK], src_p[:, HIST_P:], 1.0 / w, pool_p[:, g, HIST_P:], ALU.mult, ALU.subtract))
                step(TT(diff_T[:, g, 0:HIST_P], src_p[:, HIST_P:2 * HIST_P], inv_count[:, g, :], ALU.mult))
                step(TT(diff_T[:, g, 0:HIST_P], diff_T[:, g, 0:HIST_P], pool_p[:, g, HIST_P:2 * HIST_P], ALU.subtract))
                signal(STT(by_seq(diff_T[:, g, NP_TOK:]), src_s[:, :, HIST_P:], 1.0 / w, pool_s[:, g, :, HIST_P:],
                           ALU.mult, ALU.subtract), diff_ready, g + 1)
            for b in range(4):
                wait_read(dve, f"proj{b}")
                yp, ys = y_in_T[:, b, 0:NP_TOK], by_seq(y_in_T[:, b, NP_TOK:])
                tap = lambda j: chan[:, 4 * j + b:4 * j + b + 1]
                step(TS(yp, z_p[:, b, 0:NP_TOK], tap(0), None, ALU.mult))
                step(TS(ys, z_s[:, b, :, 0:TSEQ], tap(0), None, ALU.mult))
                for j in (1, 2):
                    step(STT(yp, z_p[:, b, j:j + NP_TOK], tap(j), yp, ALU.mult, ALU.add))
                    step(STT(ys, z_s[:, b, :, j:j + TSEQ], tap(j), ys, ALU.mult, ALU.add))
                signal(TT(y_in_T[:, b, :], y_in_T[:, b, :], b_T[:, b, :], ALU.mult), conv_ready, b + 1)
            for g in range(4):
                ps = wait_full(dve, f"pool{g}")
                free(f"pool{g}", TS(yg_T[:, g, :], ps[:, 0:NT], chan[:, 12 + g:13 + g], None, ALU.mult))
            ada(1)
            ada(2)
            for m in range(KC):
                ps = wait_full(dve, f"out_a{m}")
                wait_read(dve, f"proj{16 + m}")
                free(f"out_a{m}", TT(ga_T[:, m, :], ga_T[:, m, :], ps[:, 0:NT], ALU.mult))
            for m in range(KC):
                ps = wait_full(dve, f"out_b{m}")
                wait_read(dve, f"proj{24 + m}")
                step(TT(gb_T[:, m, :], gb_T[:, m, :], ps[:, 0:NT], ALU.mult))
                free(f"out_b{m}", TT(ga_T[:, m, :], ga_T[:, m, :], gb_T[:, m, :], ALU.add))
            step(v.memset(Y, 0.0))

            normed = [0]

            def normalise(row):
                r = row.shape[0]
                step(v.bn_stats(stats[0:r, 0:6], row[:, 0:512]))
                step(v.bn_stats(stats[0:r, 6:12], row[:, 512:]))
                step(v.bn_aggr(aggr[0:r, :], stats[0:r, :]))
                normed[0] += 1
                signal(TS(aggr[0:r, 1:2], aggr[0:r, 1:2], EPS, None, ALU.add), var_ready, normed[0])
                dve.wait_ge(sqrt_ready, normed[0])
                step(v.reciprocal(rstd[0:r, :], rstd[0:r, :]))
                step(STT(rstd2[0:r, :], rstd[0:r, :], rstd[0:r, :], aggr[0:r, 1:2], ALU.mult, ALU.mult))
                step(TS(rstd2[0:r, :], rstd2[0:r, :], -0.5, 1.5, ALU.mult, ALU.add))
                step(TT(rstd[0:r, :], rstd[0:r, :], rstd2[0:r, :], ALU.mult))
                signal(STT(shift[0:r, :], aggr[0:r, 0:1], -1.0, rstd[0:r, :], ALU.mult, ALU.mult), rstd_ready, normed[0])

            dve.wait_ge(norm1_landed, 16 * (3 + NSEQ))
            for i, r in ((0, P), (1, NS_TOK)):
                vec = ring[0:r, i, 0:3 * D].rearrange("p (i d) -> p i d", i=3)
                tmp = ln_rows[0:r, :]
                step(STT(tmp, vec[:, 2, :], 1.0, ring[0:r, 1, 3 * D:], ALU.add, ALU.mult))
                step(TT(vec[:, 1, :], vec[:, 1, :], tmp, ALU.add))
                step(STT(vec[:, 2, :], vec[:, 2, :], 1.0, ring[0:r, 0, 3 * D:], ALU.add, ALU.mult))
            dve.wait_ge(x_landed, 64)
            dve.wait_ge(out_stored, 64)
            for t in range(3):
                r = ROWS[t]
                vec = ring[0:r, 0 if t < 2 else 1, 0:3 * D].rearrange("p (i d) -> p i d", i=3)
                row = ln_rows[0:r, :]
                if t < 2:
                    for h in range(2):
                        ps = wait_full(dve, f"o{t}{h}")
                        free(f"o{t}{h}", TT(row[:, h * 512:(h + 1) * 512], ps[0:r, :], vec[:, 0, h * 512:(h + 1) * 512], ALU.mult))
                else:
                    dve.wait_ge(o2_moved, 1)
                    ps = wait_full(dve, "o2")
                    free("o2", TT(row[:, 0:512], ps[0:r, :], vec[:, 0, 0:512], ALU.mult))
                    step(TT(row[:, 512:], row[:, 512:], vec[:, 0, 512:], ALU.mult))
                step(STT(hx[0:r, t, :], hx[0:r, t, :], ALPHA, row, ALU.mult, ALU.add))
                normalise(hx[0:r, t, :])
                dve.wait_ge(row_normed, t + 1)
                step(TT(V[0:r, t, :], hx[0:r, t, :], vec[:, 2, :], ALU.mult))
                signal(TT(V[0:r, t, :], V[0:r, t, :], vec[:, 1, :], ALU.add), v_ready, t + 1)

            signal(v.memset(O_rows, 0.0), O_cleared, 1)
            dve.wait_ge(router_landed, 32)
            step(v.memset(L, 0.0))
            step(v.memset(top, 0.0))
            step(v.memset(top_f, 0.0))
            for t in range(3):
                r = ROWS[t]
                ps = wait_full(dve, f"logits{t}")
                free(f"logits{t}", TT(L[0:r, t, :], ps[0:r, 0:E], b_router[0:r, :], ALU.add))
                step(v.max(top[0:r, t, :], L[0:r, t, :]))
                step(v.max_index(top_index[0:r, t, :], top[0:r, t, :], L[0:r, t, :]))
                step(v.tensor_copy(top_f[0:r, t, :], top_index[0:r, t, :]))
            by_e = lambda t: t.to_broadcast([P, 3, E])
            experts = iota[:, 0:E].unsqueeze(1).to_broadcast([P, 3, E])
            signal(TT(eq, L, by_e(top[:, :, 0:1]), ALU.subtract), logit_ready, 1)
            step(TT(mask, experts, by_e(top_f[:, :, 0:1]), ALU.is_equal))
            dve.wait_ge(exp_ready, 1)
            for k in range(1, TOPK):
                step(TT(eq, experts, by_e(top_f[:, :, k:k + 1]), ALU.is_equal))
                ins = TT(mask, mask, eq, ALU.add)
                step(ins) if k < TOPK - 1 else signal(ins, mask_ready, 1)
            step(TT(gate, gate, mask, ALU.mult))
            step(v.reduce_sum(gsum, gate, AX_X))
            step(v.reciprocal(gsum, gsum))
            signal(TT(gate, gate, by_e(gsum.unsqueeze(2)), ALU.mult), softmax_ready, 1)
            ps = wait_full(dve, "rank")
            step(v.memset(rank, -1.0))
            for t in range(3):
                r = ROWS[t]
                ins = STT(rank[0:r, t, :], ps[0:r, t * E:(t + 1) * E], 1.0, mask[0:r, t, :], ALU.add, ALU.mult)
                step(ins) if t < 2 else free("rank", ins)
            for t in range(3):
                step(TS(rank[0:ROWS[t], t, :], rank[0:ROWS[t], t, :], -1.0, None, ALU.add))
            ps = wait_full(dve, "counts")
            free("counts", v.tensor_copy(count[0:E, :], ps[0:E, 0:1]))
            step(TS(rounds[0:E, :], count[0:E, :], float(SLOTS), 1.0, ALU.is_gt, ALU.add))
            for i in range(2, MAXR):
                ins = STT(rounds[0:E, :], count[0:E, :], float(i * SLOTS), rounds[0:E, :], ALU.is_gt, ALU.add)
                step(ins) if i < MAXR - 1 else signal(ins, rounds_ready, 1)
            ps = wait_full(dve, "bounds")
            free("bounds", v.tensor_copy(bound[0:E, :], ps[0:E, 0:1]))
            signal(TS(passed[0:E, :], iota[0:E, 0:NROUND], bound[0:E, :], None, ALU.is_ge), passed_ready, 1)
            ps = wait_full(dve, "table")
            step(TS(table[0:1, 0:NROUND], ps[0:1, 0:NROUND], float(E - 1), None, ALU.min))
            step(TT(base_f[0:1, :], iota[0:1, 0:NROUND], ps[0:1, NROUND:2 * NROUND], ALU.subtract))
            step(TS(table[0:1, NROUND:2 * NROUND], base_f[0:1, :], float(SLOTS), None, ALU.mult))
            free("table", v.tensor_copy(table[0:1, 2 * NROUND:2 * NROUND + E], ps[0:1, 2 * NROUND:2 * NROUND + E]))
            step(v.memset(S_gate, 0.0))
            step(v.memset(P_gate, 0.0))
            signal(v.memset(stats[0:1, 0:1], 0.0), table_ready, 1)
            ps = wait_full(dve, "gate_T")
            free("gate_T", v.tensor_copy(P_gate[0:E, :], ps[0:E, 0:NT]))
            dve.wait_ge(b_down_landed, 16)
            signal(v.memset(stats[0:1, 0:1], 0.0), Pg_ready, 1)
            signal(v.memset(stats[0:1, 0:1], 0.0), O_ready, 1)
            signal(v.memset(stats[0:1, 0:1], 0.0), O_ready, 2)

            G = dve.value_load(table[0:1, 159:160], min_val=1, max_val=52)

            by_slot = lambda t: t.to_broadcast([P, 3, SLOTS])

            def one_hots(n, e, base):
                slots = iota[:, bass.ds(base, SLOTS)].unsqueeze(1).to_broadcast([P, 3, SLOTS])
                signal(TT(S, slots, by_slot(rank[:, :, bass.ds(e, 1)]), ALU.is_equal), S_ready, n + 1)

            def select_bias(n, e):
                signal(v.tensor_copy(up_sel, sel3[:, bass.ds(e, 1)].to_broadcast([P, SLOTS])), sel_ready, n + 1)

            def gated(n, e):
                signal(TT(S_gate[:, :, 0:SLOTS], S, by_slot(gate[:, :, bass.ds(e, 1)]), ALU.mult), gate_ready, n + 1)

            def add_up(n):
                used = {6: 0, 7: 0}
                for i, b in enumerate(COMBINE_BANKS):
                    used[b] += 1
                    value = front_uses(b) + PER_ROUND[b] * n + used[b]
                    dve.wait_ge(bank_full[b], value)
                    signal(TT(Y[:, i, :], Y[:, i, :], bank[b][:, :], ALU.add), bank_free[b], value)

            e0 = dve.value_load(table[0:1, 0:1], min_val=0, max_val=E - 1)
            one_hots(0, e0, 0)
            select_bias(0, e0)
            gated(0, e0)
            before = steps[0]
            PER_LOOP = 2
            with dve.Fori(0, G) as g:
                steps[0] = 0
                origin[0] = g * PER_LOOP + before
                e = dve.value_load(table[0:1, bass.ds(g + 1, 1)], min_val=0, max_val=E - 1)
                base = dve.value_load(table[0:1, bass.ds(g + NROUND + 1, 1)], min_val=0, max_val=(MAXR - 1) * SLOTS)
                dve.wait_ge(bank_full[B_X], g + front_uses(B_X) + 1)
                one_hots(g + 1, e, base)
                for j in range(2):
                    b = B_UP[j]
                    dve.wait_ge(bank_full[b], g + front_uses(b) + 1)
                    signal(TS(glu[:, j, :], bank[b][:, 0:256], LIMIT, None, ALU.min), glu_ready, 2 * g + j + 1)
                    signal(TS(lin[:, j, :], bank[b][:, 256:512], -LIMIT, LIMIT, ALU.max, ALU.min), bank_free[b],
                           g + front_uses(b) + 1)
                    step(STT(lin[:, j, :], lin[:, j, :], 1.0, glu[:, j, :], ALU.add, ALU.mult))
                    dve.wait_ge(sig_ready, 2 * g + j + 1)
                    signal(TT(act_rows[:, j * 256:(j + 1) * 256], lin[:, j, :], sig[:, j, :], ALU.mult), act_ready, 2 * g + j + 1)
                select_bias(g + 1, e)
                add_up(g)
                dve.wait_ge(bank_full[B_T], g * 2 + front_uses(B_T) + 2)
                gated(g + 1, e)
                assert steps[0] == PER_LOOP
            steps[0], origin[0], step_sem[0] = 0, 0, tail_step
            dve.wait_ge(tail_landed, 16 * (3 + NSEQ))
            dve.wait_ge(h_ready, 3)
            dve.wait_ge(bank_full[B_X], G + front_uses(B_X) + 1)
            step(v.tensor_copy(Y_2[0:NS_TOK, :], Y[64:P, 4, :]))
            gate2 = lambda t, h: tail_rows[0:ROWS[t], (0 if t < 2 else D) + h * 512:(0 if t < 2 else D) + (h + 1) * 512]
            for t in range(3):
                r = ROWS[t]
                for h in range(2):
                    f = Y[0:r, 2 * t + h, :] if t < 2 else (Y[0:r, 4, :], Y_2[0:r, :])[h]
                    step(TT(V[0:r, t, h * 512:(h + 1) * 512], f, gate2(t, h), ALU.mult))
                step(TT(V[0:r, t, :], V[0:r, t, :], hx[0:r, t, :], ALU.add))
            used = {6: 0, 7: 0}
            for t in range(3):
                r = ROWS[t]
                for h in range(2):
                    i = 2 * t + h
                    if i < 5:
                        b = COMBINE_BANKS[i]
                        used[b] += 1
                        value = G * PER_ROUND[b] + (front_uses(b) + used[b])
                        dve.wait_ge(bank_full[b], value)
                        if i == 4:
                            dve.wait_ge(o2_moved, 2)
                        signal(TT(Y[0:r, i, :], bank[b][0:r, :], gate2(t, h), ALU.mult), bank_free[b], value)
                        share = Y[0:r, i, :]
                    else:
                        step(TT(y2_rows[0:r, :], y2_rows[0:r, :], gate2(t, h), ALU.mult))
                        share = y2_rows[0:r, :]
                    half = V[0:r, t, h * 512:(h + 1) * 512]
                    step(TT(half, half, share, ALU.add))
                normalise(V[0:r, t, :])
            r = ROWS[2]
            dve.wait_ge(row_normed, 6)
            step(TT(V[0:r, 2, :], V[0:r, 2, :], tail_rows[0:r, 2 * D:3 * D], ALU.mult))
            signal(TT(V[0:r, 2, :], V[0:r, 2, :], tail_rows[0:r, 3 * D:], ALU.add), y_ready, 1)


INPUTS = ["x_prompt", "x_sample", "c_prompt", "c_sample", "state_conv", "state_pool", "w_ada", "b_ada", "w_in",
          "conv_w", "w_out_a", "w_pool", "ls_pool", "w_out_b", "w_o", "ln1_g", "ln1_b", "w_router", "b_router",
          "w_up", "b_up", "w_down", "b_down", "ln2_g", "ln2_b"]
OUTPUTS = {"y_p": (1, NP_TOK, D), "y_s": (NSEQ, TSEQ, D), "conv_p": (1, 1, HIST_C, DC), "pool_p": (1, 1, HIST_P, DC),
           "conv_s": (1, NSEQ, HIST_C, DC), "pool_s": (1, NSEQ, HIST_P, DC)}


def constants():
    c = np.zeros((P, C_N), np.float32)
    c[:, C_ID:C_ID + P] = np.eye(P)
    c[:, C_TRI:C_TRI + P] = np.triu(np.ones((P, P)), 1)
    c[:, C_ONE:C_ONE + P] = 1.0
    c[:, C_TRI1:C_TRI1 + E] = np.triu(np.ones((P, E)))
    c[:, C_IOTA:C_IOTA + NT] = np.arange(NT)
    for g, w in enumerate(WINDOWS):
        c[:, C_INV + g * HIST_P:C_INV + (g + 1) * HIST_P] = 1.0 / np.minimum(w, np.arange(HIST_P) + 1)
    for q in range(3):
        c[32 * q:32 * q + E, C_SEL:C_SEL + E] = np.eye(E)
    return c


def kernel(**inputs):
    import concourse.bacc as bacc
    from concourse.bass_utils import run_bass_kernel_spmd

    nc = bacc.Bacc("TRN2", target_bir_lowering=False, num_devices=1)
    arrays = {f"in_{n}": np.ascontiguousarray(inputs[n]) for n in INPUTS}
    arrays["in_const"] = constants()
    a = {n: nc.dram_tensor(f"in_{n}", arrays[f"in_{n}"].shape, F32, kind="ExternalInput").ap() for n in INPUTS + ["const"]}
    o = {n: nc.dram_tensor(f"out_{n}", shape, F32, kind="ExternalOutput").ap() for n, shape in OUTPUTS.items()}
    program(nc, a, o)
    r = run_bass_kernel_spmd(nc, [arrays], core_ids=[0]).results[0]
    return tuple(r[f"out_{n}"] for n in OUTPUTS)
```

```python
from contextlib import ExitStack

import numpy as np

import concourse.bass as bass
from concourse import mybir

F32R = mybir.dt.float32r
F32 = mybir.dt.float32
BF16 = mybir.dt.bfloat16
I32 = mybir.dt.int32
U32 = mybir.dt.uint32
ALU = mybir.AluOpType
ACT = mybir.ActivationFunctionType
AX_X = mybir.AxisListType.X

P = 128
D = 1024
DC = 512
KC = D // P
NP_TOK = 256
NSEQ, TSEQ = 8, 8
NS_TOK = NSEQ * TSEQ
NT = NP_TOK + NS_TOK
ROWS = (P, P, NS_TOK)
NC_ROWS = 1 + NSEQ
HIST_C, HIST_P = 2, 15
WINDOWS = (2, 4, 8, 16)
E = 32
TOPK = 4
SLOTS = 64
MAXR = -(-NT // SLOTS)
NROUND = 64
LIMIT, SWISH = 7.0, 1.702
EPS = 1e-5
ALPHA = 2.0 ** 0.25

C_ID, C_TRI, C_ONE, C_TRI1, C_IOTA, C_INV = 0, 128, 256, 384, 416, 736
C_SEL = C_INV + 4 * HIST_P
C_N = C_SEL + E

RING = 6
CH = 4096
FRONT_N = 18720
EXPERT_CHUNKS = 6
FRONT_CHUNKS = 24
FRONT_SLOT = (0, 1, 2, 3) + (4, 5, 0, 1, 4, 5, 0, 1) + (4, 5, 0, 2) + (1, 3) + (4, 5, 0, 2) + (1, 4)
HIGH_SLOT = (2, 3)
ROW_SLOT = (5, 0)
EXPERT_SLOT = (2, 3, 1, 4, 5, 0)

FRONT = (
    ["c_T", "chan_T"] + ["ada0"] + [f"x_T{k}" for k in range(4)] + ["mod_T"] + [f"x_T{k}" for k in range(4, KC)]
    + [f"proj{m}" for m in (4, 5, 6, 7)] + ["conv_hist_T", "pool_hist_T"] + [f"proj{m}" for m in (8, 9, 10, 11, 0, 1, 2, 3, 12, 13, 14, 15)]
    + [f"proj{m}" for m in range(16, 32)]
    + [f"pool{g}" for g in range(4)]
    + ["state_cp", "state_cs", "state_pp", "state_ps"]
    + ["ada1"] + [f"out_a{m}" for m in range(8)]
    + [f"out_b{m}" for m in range(4)] + ["ada2"] + [f"out_b{m}" for m in range(4, 8)]
    + ["o00", "o01", "o2", "o10", "o11", "v_T00", "v_T01", "logits0", "v_T20", "v_T21", "logits2", "v_T10", "v_T11",
       "logits1", "rank", "counts", "bounds", "table", "gate_T"]
)
B_UP, B_X, B_DOWN, B_T, B_XT, B_C = (0, 1), 3, 2, 4, 5, (6, 7)
COMBINE_BANKS = (6, 7, 6, 7, 6)
PER_ROUND = [1, 1, 1, 1, 2, 1, 3, 2]


TILE_ORDER = (0, 2, 1)


def front_place(name):
    n = FRONT.index(name)
    return n % 8, n // 8


def front_uses(bank):
    return len([n for n in range(len(FRONT)) if n % 8 == bank])


def program(nc, a, o):
    ctx = ExitStack()
    with ctx:
        def sb(name, shape, dt=F32):
            return ctx.enter_context(nc.sbuf_tensor(name, shape, dt))

        def sem(name):
            return ctx.enter_context(nc.semaphore(name))

        start = -(-nc.sbuf_base // 32) * 32
        ring = sb("ring", [P, RING, CH])
        front = sb("front", [P, FRONT_N])
        hx = sb("hx", [P, 3, D])
        tail_rows = sb("tail_rows", [P, 4 * D])
        const = sb("const", [P, C_N])
        small = sb("small", [P, 700])
        table = sb("table", [1, 192], I32)
        top_index = sb("top_index", [P, 3, 8], U32)
        mod_rows = nc.dram_tensor("mod_rows", [NC_ROWS, 6 * D], F32)
        bank = [ctx.enter_context(nc.psum_tensor(f"bank{b}", [P, 512], F32)) for b in range(8)]

        def region(t, at, *shape):
            n = int(np.prod(shape))
            v = t[:, at:at + n]
            if len(shape) == 2:
                return v.rearrange("p (a b) -> p a b", a=shape[0])
            if len(shape) == 3:
                return v.rearrange("p (a b c) -> p a b c", a=shape[0], b=shape[1])
            return v

        ident = const[:, C_ID:C_ID + P]
        tri = const[:, C_TRI:C_TRI + P]
        ones = const[:, C_ONE:C_ONE + P]
        tri_incl = const[:, C_TRI1:C_TRI1 + E]
        iota = const[:, C_IOTA:C_IOTA + NT]
        sel3 = const[:, C_SEL:C_SEL + E]
        inv_count = region(const, C_INV, 4, HIST_P)

        u_T = region(front, 0, KC, NT)
        ring_parts = nc.alloc_sbuf_tensor_at("ring_parts", [P, RING, CH], F32R, offset=start)
        u_low = nc.alloc_sbuf_tensor_at("u_low", [P, KC, NT], F32R, offset=start + 4 * RING * CH)
        u_high = nc.alloc_sbuf_tensor_at("u_high", [P, KC, NT], F32R, offset=start + 4 * (RING * CH + FRONT_N))
        b_T = region(front, 2560, 4, NT)
        c_T = region(front, 3840, 4, NT)
        z_p = region(front, 5120, 4, HIST_C + NP_TOK)
        z_s = region(front, 6152, 4, NSEQ, HIST_C + TSEQ)
        pool_p = region(front, 6472, 4, HIST_P + NP_TOK)
        pool_s = region(front, 7556, 4, NSEQ, HIST_P + TSEQ)
        diff_T = region(front, 8292, 4, NT)
        y_in_T = region(front, 9572, 4, NT)
        yg_T = region(front, 10852, 4, NT)
        ga_T = region(front, 12132, KC, NT)
        gb_T = region(front, 14692, KC, NT)
        sum_p = region(front, 17252, 2, HIST_P + NP_TOK)
        sum_s = region(front, 17800, 2, NSEQ, HIST_P + TSEQ)
        keep_s = region(front, 18168, 4, NSEQ, HIST_C)
        keep_ps = region(front, 18232, 4, NSEQ, HIST_P)
        c_rows = region(front, 12132, D)
        chan_rows = region(front, 13156, P)
        conv_hist = region(front, 10852, DC)
        pool_hist = region(front, 11364, DC)
        mod = region(tail_rows, 0, 3, 512)
        b_ada_rows = region(tail_rows, 1536, 3, 512)
        sg_c = region(small, 0, KC, NC_ROWS)
        sc_T = region(small, 72, KC, NC_ROWS)
        chan = region(small, 144, 16)
        state_rows = region(front, 0, 4, DC)
        V = region(front, 0, 3, D)
        b_up_rows = region(front, 3072, 2 * D)
        norm1_rows = region(front, 3072, 2, D)
        b_up_parts = region(front, 5120, D).bitcast(BF16)
        v_T = region(front, 8292, KC, NT)
        S = region(front, 6472, 3, SLOTS)
        S_gate = region(front, 6664, 3, P)
        x_rows = region(front, 7048, 512)
        up_sel = region(front, 7560, SLOTS // 2).bitcast(BF16)
        glu = region(front, 8292, 2, 256)
        lin = region(front, 8804, 2, 256)
        sig = region(front, 9316, 2, 256)
        act_rows = region(front, 9828, 512)
        act_T = region(front, 10340, 4, P)
        x_T = region(front, 10852, 4, P)
        P_gate = region(front, 11364, NT)
        O_rows = region(front, 11684, 2, 512)
        Y = region(front, 14692, 5, 512)
        y2_rows = region(front, 12708, 512)
        Y_2 = region(front, 13220, 512)
        w_pool = region(small, 160, 4, P)
        w_router = region(small, 160, KC, E)
        b_router = region(small, 672 - 256, E)
        mod_T = region(front, 17252 - 0, 4, P)
        stats = region(front, 17252, 12)
        aggr = region(front, 17264, 2)
        rstd = region(front, 17266, 1)
        ln_rows = region(front, 10852, D)
        ab_rows = region(front, 8292, D)
        rstd2 = region(front, 17267, 1)
        shift = region(front, 17268, 1)
        L = region(front, 17272, 3, E)
        top = region(front, 17368, 3, 8)
        top_f = region(front, 17392, 3, 8)
        mask = region(front, 17416, 3, E)
        eq = region(front, 17512, 3, E)
        gate = region(front, 17608, 3, E)
        gsum = region(front, 17704, 3)
        rank = region(front, 17707, 3, E)
        count = region(front, 17803, 1)
        rounds = region(front, 17804, 1)
        bound = region(front, 17805, 1)
        passed = region(front, 17806, NROUND)
        base_f = region(front, 17870, NROUND)

        bank_full = [sem(f"bank_full{b}") for b in range(8)]
        bank_free = [sem(f"bank_free{b}") for b in range(8)]
        chunk_landed = [sem(f"chunk_landed{s}") for s in range(RING)]
        chunk_used = [sem(f"chunk_used{s}") for s in range(RING)]
        const_landed = sem("const_landed")
        rows_landed = sem("rows_landed")
        x_landed = sem("x_landed")
        hist_landed = sem("hist_landed")
        bada_landed = sem("bada_landed")
        pool_w_landed = sem("pool_w_landed")
        router_landed = sem("router_landed")
        norm1_landed = sem("norm1_landed")
        tail_landed = sem("tail_landed")
        bias_landed = sem("bias_landed")
        mod_stored = sem("mod_stored")
        out_stored = sem("out_stored")
        dve_step = sem("dve_step")
        tail_step = sem("tail_step")
        c_sig_ready = sem("c_sig_ready")
        diff_ready = sem("diff_ready")
        conv_ready = sem("conv_ready")
        v_ready = sem("v_ready")
        keep_ready = sem("keep_ready")
        logit_ready = sem("logit_ready")
        var_ready = sem("var_ready")
        w_high_ready = sem("w_high_ready")
        w_low_ready = sem("w_low_ready")
        u_high_ready = sem("u_high_ready")
        u_low_ready = sem("u_low_ready")
        sqrt_ready = sem("sqrt_ready")
        scale2_landed = [sem("scale2_prompt_landed"), sem("scale2_sample_landed")]
        sqrt_table = sem("sqrt_table")
        rstd_ready = sem("rstd_ready")
        row_normed = sem("row_normed")
        o2_moved = sem("o2_moved")
        norm1_again = sem("norm1_again")
        h_step = sem("h_step")
        h_ready = sem("h_ready")
        exp_ready = sem("exp_ready")
        mask_ready = sem("mask_ready")
        rounds_ready = sem("rounds_ready")
        passed_ready = sem("passed_ready")
        table_ready = sem("table_ready")
        parts_step = sem("parts_step")
        b_up_ready = sem("b_up_ready")
        b_down_landed = sem("b_down_landed")
        O_cleared = sem("O_cleared")
        softmax_ready = sem("softmax_ready")
        sel_ready = sem("sel_ready")
        S_ready = sem("S_ready")
        gate_ready = sem("gate_ready")
        x_rows_ready = sem("x_rows_ready")
        xT_ready = sem("xT_ready")
        glu_ready = sem("glu_ready")
        sig_ready = sem("sig_ready")
        act_ready = sem("act_ready")
        actT_ready = sem("actT_ready")
        Pg_ready = sem("Pg_ready")
        O_ready = sem("O_ready")
        y_ready = sem("y_ready")

        block = ctx.enter_context(nc.Block())

        def front_slot(n):
            return FRONT_SLOT[n]

        def in_slot(n):
            return [m for m in range(n + 1) if front_slot(m) == front_slot(n)]

        def last_in_slot(s):
            return max(n for n in range(FRONT_CHUNKS) if front_slot(n) == s)

        def expert_slot(c):
            return EXPERT_SLOT[c]

        def landed_before(s):
            return FRONT_SLOT.count(s)

        def last_result(n):
            if n in (3, 15, 21):
                return f"ada{(3, 15, 21).index(n)}"
            if 4 <= n < 12:
                return f"proj{4 * IN_ORDER[n - 4] + 3}"
            return {16: "out_a7", 17: "out_b7", 23: "o11"}.get(n)

        def used_before(s):
            return len([n for n in range(FRONT_CHUNKS) if front_slot(n) == s and last_result(n) is None])

        def wait_chunk_read(eng, n):
            if last_result(n) is None:
                eng.wait_ge(chunk_used[front_slot(n)], len([m for m in in_slot(n) if last_result(m) is None]))
            else:
                wait_full(eng, last_result(n))

        IN_ORDER = (1, 2, 0, 3, 4, 5, 6, 7)
        ADA_CHUNK = [0, 12, 18]
        IN_CHUNK, OUTA_CHUNK, OUTB_CHUNK, O_CHUNK = 4, 16, 17, 22

        LAST_PROJ = f"proj{4 * IN_ORDER[7] + 3}"

        def wait_full(eng, name):
            b, n = front_place(name)
            eng.wait_ge(bank_full[b], n + 1)
            return bank[b]

        def wait_read(eng, name):
            b, n = front_place(name)
            eng.wait_ge(bank_free[b], n + 1)

        @block.sync
        def _(sp):
            w_ada = a["w_ada"][0].rearrange("(k p) n -> p k n", p=P)
            w_in = a["w_in"][0].rearrange("(k p) n -> p k n", p=P)

            def front_chunk(n, src, shape):
                s = front_slot(n)
                if s in HIGH_SLOT and len(in_slot(n)) == 2:
                    wait_chunk_read(sp, 10 + HIGH_SLOT.index(s))
                if len(in_slot(n)) > 1:
                    wait_chunk_read(sp, in_slot(n)[-2])
                dst = ring[:, s, :].rearrange("p (a b) -> p a b", a=shape[0])
                sp.dma_start(dst, src).then_inc(chunk_landed[s], 16)

            sp.dma_start(const[:, :], a["const"]).then_inc(const_landed, 16)
            sp.dma_start(c_rows[0:1, :], a["c_prompt"]).then_inc(rows_landed, 16)
            sp.dma_start(c_rows[1:NC_ROWS, :], a["c_sample"]).then_inc(rows_landed, 16)
            sp.dma_start(chan_rows[0:12, :], a["conv_w"][0].rearrange("j (b i) -> (j b) i", i=P)).then_inc(rows_landed, 16)
            sp.dma_start(chan_rows[12:16, :], a["ls_pool"][0].rearrange("(b i) -> b i", i=P)).then_inc(rows_landed, 16)
            for i in range(4):
                front_chunk(ADA_CHUNK[0] + i, w_ada[:, 2 * i:2 * i + 2, 0:2048], (2, 2048))
                if i == 2:
                    for q in range(4):
                        src = a["b_ada"][0].rearrange("(n q m) -> n q m", n=3, q=4)[:, q, :]
                        sp.dma_start(b_ada_rows[32 * q:32 * q + NC_ROWS, :, :], src.partition_broadcast(NC_ROWS)).then_inc(bada_landed, 16)
                if i == 3:
                    sp.dma_start(hx[:, 0:2, :], a["x_prompt"][0].rearrange("(t p) d -> p t d", p=P)).then_inc(x_landed, 16)
                    sp.dma_start(hx[0:NS_TOK, 2, :], a["x_sample"].rearrange("s t d -> (s t) d")).then_inc(x_landed, 16)
            for i in range(8):
                m = IN_ORDER[i]
                front_chunk(IN_CHUNK + i, w_in[:, :, m * 512:(m + 1) * 512], (8, 512))
                if i == 1:
                    sp.dma_start(conv_hist[0:NSEQ * HIST_C, :], a["state_conv"][0].rearrange("s t d -> (s t) d")).then_inc(hist_landed, 16)
                    sp.dma_start(pool_hist[0:NSEQ * HIST_P, :], a["state_pool"][0].rearrange("s t d -> (s t) d")).then_inc(hist_landed, 16)
            def store_mod(n):
                wait_read(sp, f"ada{n}")
                for q in range(4):
                    sp.dma_start(mod_rows[:, n * 2048 + q * 512:n * 2048 + (q + 1) * 512],
                                 mod[32 * q:32 * q + NC_ROWS, n, :]).then_inc(mod_stored, 16)

            def ada_chunks(third):
                for i in range(4):
                    front_chunk(ADA_CHUNK[third] + i,
                                w_ada[:, 2 * i:2 * i + 2, third * 2048:(third + 1) * 2048], (2, 2048))

            store_mod(0)
            ada_chunks(1)
            front_chunk(OUTA_CHUNK, a["w_out_a"][0].rearrange("(k p) n -> p k n", p=P), (4, D))
            front_chunk(OUTB_CHUNK, a["w_out_b"][0].rearrange("(k p) n -> p k n", p=P), (4, D))
            wait_full(sp, LAST_PROJ)
            sp.dma_start(hx[:, 0:2, :], a["x_prompt"][0].rearrange("(t p) d -> p t d", p=P)).then_inc(x_landed, 16)
            sp.dma_start(hx[0:NS_TOK, 2, :], a["x_sample"].rearrange("s t d -> (s t) d")).then_inc(x_landed, 16)
            ada_chunks(2)
            store_mod(1)
            for i in range(2):
                front_chunk(O_CHUNK + i, a["w_o"][0, i * 512:(i + 1) * 512, :].rearrange("(k p) n -> p k n", p=P),
                            (4, D))
            for r in ROW_SLOT:
                wait_chunk_read(sp, last_in_slot(r))
            sp.wait_ge(mod_stored, 16 * 8)

            def mod_for_tokens(at, to, prompt_landed, sample_landed):
                lo, hi = at - 2 * D, to - 2 * D
                sp.dma_start(ring[:, ROW_SLOT[0], lo:hi], mod_rows[0, at:to].partition_broadcast(P)).then_inc(prompt_landed, 16)
                for s in range(NSEQ):
                    sp.dma_start(ring[TSEQ * s:TSEQ * (s + 1), ROW_SLOT[1], lo:hi],
                                 mod_rows[1 + s, at:to].partition_broadcast(TSEQ)).then_inc(sample_landed, 16)

            sp.dma_start(ring[:, ROW_SLOT[0], 3 * D:], a["ln1_g"][0].partition_broadcast(P)).then_inc(norm1_landed, 16)
            sp.dma_start(ring[:, ROW_SLOT[1], 3 * D:], a["ln1_b"][0].partition_broadcast(P)).then_inc(norm1_landed, 16)
            mod_for_tokens(2 * D, 4 * D, norm1_landed, norm1_landed)
            store_mod(2)
            sp.wait_ge(mod_stored, 16 * 12)
            mod_for_tokens(4 * D, 5 * D, scale2_landed[0], scale2_landed[1])

            def expert_chunk(c, e):
                s = expert_slot(c)
                if c < 4:
                    j, half = divmod(c, 2)
                    for g in range(2):
                        src = a["w_up"][0][:, half * 512:(half + 1) * 512, g * D + j * 512:g * D + (j + 1) * 512]
                        sp.dma_start(ring[:, s, g * 2048:(g + 1) * 2048].rearrange("p (k m) -> p k m", k=4),
                                     src.rearrange("e (k p) m -> p e k m", p=P)[:, e]).then_inc(chunk_landed[s], 16)
                else:
                    src = a["w_down"][0][:, (c - 4) * 512:(c - 3) * 512, :].rearrange("e (k p) m -> p e k m", p=P)
                    sp.dma_start(ring[:, s, :].rearrange("p (k m) -> p k m", k=4), src[:, e]).then_inc(chunk_landed[s], 16)

            for c in range(EXPERT_CHUNKS):
                if expert_slot(c) in ROW_SLOT:
                    sp.wait_ge(v_ready, 3)
                else:
                    wait_chunk_read(sp, last_in_slot(expert_slot(c)))
                expert_chunk(c, 0)
            sp.wait_ge(table_ready, 1)
            ends_with = {1: B_UP[0], 3: B_UP[1], 5: B_DOWN}
            with sp.Fori(1, E) as e:
                rounds_done = sp.value_load(table[0:1, bass.ds(e + 127, 1)], min_val=1, max_val=52)
                for c in range(EXPERT_CHUNKS):
                    if c in ends_with:
                        b = ends_with[c]
                        sp.wait_ge(bank_full[b], rounds_done + front_uses(b))
                    else:
                        s = expert_slot(c)
                        sp.wait_ge(chunk_used[s], rounds_done + used_before(s))
                    expert_chunk(c, e)

        @block.gpsimd
        def _(pool):
            pool.dma_start(w_pool, a["w_pool"][0].rearrange("g c d -> c g d")).then_inc(pool_w_landed, 16)
            for i in range(8):
                slot = front_slot(IN_CHUNK + i)
                for q in range(4):
                    pool.wait_ge(w_high_ready, 4 * i + q + 1)
                    part = slice(q * 1024, (q + 1) * 1024)
                    pool.tensor_tensor(ring_parts[:, slot, part], ring[:, slot, part],
                                       ring_parts[:, HIGH_SLOT[i % 2], part].bitcast(F32), ALU.subtract).then_inc(w_low_ready, 1)
            for name in ("state_cp", "state_cs", "state_pp", "state_ps"):
                wait_read(pool, name)
            rows = ((o["conv_p"][0, 0], 2, 0), (o["conv_s"][0].rearrange("s t d -> (s t) d"), 16, 1),
                    (o["pool_p"][0, 0], 15, 2), (o["pool_s"][0].rearrange("s t d -> (s t) d"), 120, 3))
            for dst, n, i in rows:
                pool.dma_start(dst, state_rows[0:n, i, :]).then_inc(out_stored, 16)
            wait_full(pool, "pool3")
            pool.dma_start(w_router, a["w_router"][0].rearrange("(k p) e -> p k e", p=P)).then_inc(router_landed, 16)
            pool.dma_start(b_router, a["b_router"][0].partition_broadcast(P)).then_inc(router_landed, 16)
            wait_full(pool, "state_ps")
            pool.wait_ge(conv_ready, 4)
            for q in range(3):
                pool.dma_start(b_up_rows[32 * q:32 * q + E, :], a["b_up"][0]).then_inc(bias_landed, 16)
            done = [0]

            def part(ins):
                done[0] += 1
                ins.then_inc(parts_step, 1)
                pool.wait_ge(parts_step, done[0])

            part(pool.memset(b_up_parts, 0.0))
            pool.wait_ge(bias_landed, 48)
            part(pool.tensor_copy(b_up_parts[0:96, :], b_up_rows[0:96, :]))
            for q in (1, 2):
                rows, parts = b_up_rows[32 * q:32 * q + E, :], b_up_parts[32 * q:32 * q + E, :]
                for i in range(q):
                    part(pool.tensor_tensor(rows, rows, parts, ALU.subtract))
                    part(pool.tensor_copy(parts, rows))
            pool.memset(b_up_rows[0:1, 0:1], 0.0).then_inc(b_up_ready, 1)
            pool.wait_ge(mod_stored, 16 * 12)
            pool.dma_start(tail_rows[:, 0:D], mod_rows[0, 5 * D:].partition_broadcast(P)).then_inc(tail_landed, 16)
            for s in range(NSEQ):
                pool.dma_start(tail_rows[TSEQ * s:TSEQ * (s + 1), D:2 * D],
                               mod_rows[1 + s, 5 * D:].partition_broadcast(TSEQ)).then_inc(tail_landed, 16)
            pool.dma_start(tail_rows[:, 2 * D:3 * D], a["ln2_g"][0].partition_broadcast(P)).then_inc(tail_landed, 16)
            pool.dma_start(tail_rows[:, 3 * D:], a["ln2_b"][0].partition_broadcast(P)).then_inc(tail_landed, 16)
            pool.wait_ge(v_ready, 3)
            pool.memset(O_rows, 0.0).then_inc(O_cleared, 1)
            pool.wait_ge(O_cleared, 1)
            pool.dma_start(O_rows[0:E, :, :], a["b_down"][0].rearrange("e (h m) -> e h m", h=2)).then_inc(b_down_landed, 16)
            pool.wait_ge(b_up_ready, 1)
            pool.dma_start(norm1_rows[:, 0, :], a["ln1_g"][0].partition_broadcast(P)).then_inc(norm1_again, 16)
            pool.dma_start(norm1_rows[:, 1, :], a["ln1_b"][0].partition_broadcast(P)).then_inc(norm1_again, 16)
            pool.wait_ge(norm1_again, 32)
            for i, t in enumerate(TILE_ORDER):
                r = ROWS[t]
                row = hx[0:r, t, :]
                pool.wait_ge(v_ready, i + 1)
                pool.tensor_tensor(row, row, norm1_rows[0:r, 0, :], ALU.mult).then_inc(h_step, 1)
                pool.wait_ge(h_step, 2 * i + 1)
                pool.tensor_tensor(row, row, norm1_rows[0:r, 1, :], ALU.add).then_inc(h_step, 1)
                pool.wait_ge(h_step, 2 * i + 2)
                pool.tensor_scalar(row, row, ALPHA, 1.0, ALU.mult, ALU.mult).then_inc(h_ready, 1)
            outs = (o["y_p"][0, 0:P], o["y_p"][0, P:2 * P], o["y_s"].rearrange("s t d -> (s t) d"))
            for t in range(2):
                row = V[:, t, :]
                pool.wait_ge(row_normed, 4 + t)
                pool.tensor_tensor(row, row, tail_rows[:, 2 * D:3 * D], ALU.mult).then_inc(h_step, 1)
                pool.wait_ge(h_step, 7 + 2 * t)
                pool.tensor_tensor(row, row, tail_rows[:, 3 * D:], ALU.add).then_inc(h_step, 1)
                pool.wait_ge(h_step, 8 + 2 * t)
                pool.dma_start(outs[t], row).then_inc(out_stored, 16)
            pool.wait_ge(y_ready, 1)
            pool.dma_start(outs[2], V[0:NS_TOK, 2, :]).then_inc(out_stored, 16)
            pool.wait_ge(out_stored, 16 * 7)

        @block.tensor
        def _(pe):
            mm = nc.tensor.matmul

            def take(name):
                b, n = front_place(name)
                if n:
                    pe.wait_ge(bank_free[b], n)
                return bank[b]

            def done(name, ins):
                ins.then_inc(bank_full[front_place(name)[0]], 1)

            def chunk(n):
                s = front_slot(n)
                pe.wait_ge(chunk_landed[s], 16 * len(in_slot(n)))
                return ring[:, s, :]

            pe.wait_ge(const_landed, 16)
            pe.wait_ge(rows_landed, 64)
            ps = take("c_T")
            for k in range(KC):
                last = nc.tensor.transpose(ps[:, k * NC_ROWS:(k + 1) * NC_ROWS], c_rows[0:NC_ROWS, k * P:(k + 1) * P],
                                           ident[0:NC_ROWS, 0:NC_ROWS])
            done("c_T", last)
            ps = take("chan_T")
            done("chan_T", nc.tensor.transpose(ps[:, 0:16], chan_rows[0:16, :], ident[0:16, 0:16]))

            def ada(third):
                ps = take(f"ada{third}")
                for i in range(4):
                    w = chunk(ADA_CHUNK[third] + i).rearrange("p (a b) -> p a b", a=2)
                    for kk in range(2):
                        k = 2 * i + kk
                        for q in range(4):
                            last = mm(ps[32 * q:32 * q + NC_ROWS, :], sc_T[:, k, :], w[:, kk, q * 512:(q + 1) * 512],
                                      start=k == 0, stop=k == KC - 1)
                    if i < 3:
                        last.then_inc(chunk_used[front_slot(ADA_CHUNK[third] + i)], 1)
                done(f"ada{third}", last)

            wait_read(pe, "c_T")
            ada(0)
            pe.wait_ge(x_landed, 32)
            for k in range(KC):
                if k == 4:
                    wait_read(pe, "ada0")
                    ps = take("mod_T")
                    for blk in range(4):
                        last = nc.tensor.transpose(ps[:, blk * P:(blk + 1) * P], mod[:, 0, blk * P:(blk + 1) * P], ident)
                    done("mod_T", last)
                ps = take(f"x_T{k}")
                for t in range(3):
                    r = ROWS[t]
                    last = nc.tensor.transpose(ps[:, t * P:t * P + r], hx[0:r, t, k * P:(k + 1) * P], ident[0:r, 0:r])
                done(f"x_T{k}", last)
            def proj(i, m4):
                low = ring_parts[:, front_slot(IN_CHUNK + i), :].rearrange("p (k m) -> p k m", k=KC)
                high = ring_parts[:, HIGH_SLOT[i % 2], :].rearrange("p (k m) -> p k m", k=KC)
                blocks = [take(f"proj{4 * m4 + j}") for j in range(4)]

                def pass_over(j, w, u, k, start=False, stop=False):
                    return mm(blocks[j][:, 0:NT], w[:, k, j * P:(j + 1) * P], u[:, k, :], start=start, stop=stop)

                for j in range(4):
                    for k in range(KC):
                        if j == 0 and k % 2 == 0:
                            pe.wait_ge(w_high_ready, 4 * i + k // 2 + 1)
                        if i == 0 and j == 0:
                            pe.wait_ge(u_high_ready, k + 1)
                        pass_over(j, high, u_high, k, start=k == 0)
                for j in range(4):
                    for k in range(KC):
                        if i == 0 and j == 0:
                            pe.wait_ge(u_low_ready, k + 1)
                        pass_over(j, high, u_low, k)
                for j in range(4):
                    for k in range(KC):
                        if j == 0 and k % 2 == 0:
                            pe.wait_ge(w_low_ready, 4 * i + k // 2 + 1)
                        last = pass_over(j, low, u_high, k, stop=k == KC - 1)
                    done(f"proj{4 * m4 + j}", last)

            proj(0, IN_ORDER[0])
            pe.wait_ge(hist_landed, 32)
            for name, src, r in (("conv_hist_T", conv_hist, 16), ("pool_hist_T", pool_hist, 120)):
                ps = take(name)
                for blk in range(4):
                    last = nc.tensor.transpose(ps[:, blk * r:(blk + 1) * r], src[0:r, blk * P:(blk + 1) * P], ident[0:r, 0:r])
                done(name, last)
            for i in range(1, 8):
                proj(i, IN_ORDER[i])
            pe.wait_ge(pool_w_landed, 16)
            for g in range(4):
                pe.wait_ge(diff_ready, g + 1)
                ps = take(f"pool{g}")
                done(f"pool{g}", mm(ps[:, 0:NT], w_pool[:, g, :], diff_T[:, g, :], start=True, stop=True))

            pe.wait_ge(keep_ready, 2)
            pieces = (("state_cp", 2, lambda b: z_p[:, b, NP_TOK:]),
                      ("state_cs", 16, lambda b: keep_s[:, b, :, :].rearrange("p s t -> p (s t)")),
                      ("state_pp", 15, lambda b: pool_p[:, b, NP_TOK:]),
                      ("state_ps", 120, lambda b: keep_ps[:, b, :, :].rearrange("p s t -> p (s t)")))
            for name, r, piece in pieces:
                ps = take(name)
                for b in range(4):
                    last = nc.tensor.transpose(ps[0:r, b * P:(b + 1) * P], piece(b), ident)
                done(name, last)

            def out(name, w, y, ms):
                for m in ms:
                    ps = take(f"{name}{m}")
                    for k in range(4):
                        last = mm(ps[:, 0:NT], w[:, k, m * P:(m + 1) * P], y[:, k, :], start=k == 0, stop=k == 3)
                    done(f"{name}{m}", last)

            ada(1)
            pe.wait_ge(conv_ready, 4)
            out("out_a", chunk(OUTA_CHUNK).rearrange("p (k m) -> p k m", k=4), y_in_T, range(8))
            for g in range(4):
                wait_read(pe, f"pool{g}")
            w_out_b = chunk(OUTB_CHUNK).rearrange("p (k m) -> p k m", k=4)
            out("out_b", w_out_b, yg_T, range(4))
            ada(2)
            out("out_b", w_out_b, yg_T, range(4, 8))
            wo = [chunk(O_CHUNK + i).rearrange("p (k m) -> p k m", k=4) for i in range(2)]
            def o_prompt(t):
                for h in range(2):
                    ps = take(f"o{t}{h}")
                    for k in range(KC):
                        if t == 0 and h == 0:
                            wait_read(pe, f"out_b{k}")
                        last = mm(ps[:, :], ga_T[:, k, t * P:(t + 1) * P], wo[k // 4][:, k % 4, h * 512:(h + 1) * 512],
                                  start=k == 0, stop=k == KC - 1)
                        if t == 1 and h == 1 and k == 3:
                            last.then_inc(chunk_used[front_slot(O_CHUNK)], 1)
                    done(f"o{t}{h}", last)

            o_prompt(0)
            ps = take("o2")
            for k in range(KC):
                for h in range(2):
                    last = mm(ps[64 * h:64 * h + 64, :], ga_T[:, k, 2 * P:NT], wo[k // 4][:, k % 4, h * 512:(h + 1) * 512],
                              start=k == 0, stop=k == KC - 1)
            done("o2", last)
            o_prompt(1)

            def v_transposes(t):
                pe.wait_ge(v_ready, TILE_ORDER.index(t) + 1)
                r = ROWS[t]
                for half in range(2):
                    ps = take(f"v_T{t}{half}")
                    for i in range(4):
                        k = 4 * half + i
                        last = nc.tensor.transpose(ps[:, i * P:i * P + r], V[0:r, t, k * P:(k + 1) * P], ident[0:r, 0:r])
                    done(f"v_T{t}{half}", last)

            def logits(t):
                ps = take(f"logits{t}")
                for k in range(KC):
                    if k % 4 == 0:
                        wait_read(pe, f"v_T{t}{k // 4}")
                    last = mm(ps[0:ROWS[t], 0:E], v_T[:, k, t * P:t * P + ROWS[t]], w_router[:, k, :],
                              start=k == 0, stop=k == KC - 1)
                done(f"logits{t}", last)

            pe.wait_ge(router_landed, 32)
            for t in TILE_ORDER:
                v_transposes(t)
                logits(t)

            def gather(n, x_rows_read=None):
                pe.wait_ge(S_ready, n + 1)
                if x_rows_read is not None:
                    pe.wait_ge(x_rows_ready, x_rows_read)
                for t in range(3):
                    for h in range(2):
                        last = mm(bank[B_X][64 * h:64 * h + 64, :], S[0:ROWS[t], t, :], V[0:ROWS[t], t, h * 512:(h + 1) * 512],
                                  start=t == 0, stop=t == 2)
                last.then_inc(bank_full[B_X], 1)

            def x_transposes(n, xT_read=None):
                pe.wait_ge(x_rows_ready, n + 1)
                if xT_read is not None:
                    pe.wait_ge(xT_ready, xT_read)
                for q in range(4):
                    last = nc.tensor.transpose(bank[B_XT][:, q * P:(q + 1) * P], x_rows[:, q * P:(q + 1) * P], ident)
                last.then_inc(bank_full[B_XT], 1)

            pe.wait_ge(mask_ready, 1)
            ps = take("rank")
            for t in range(3):
                for i in range(t + 1):
                    lhs = tri if i == t else ones
                    last = mm(ps[0:ROWS[t], t * E:(t + 1) * E], lhs[0:ROWS[i], 0:ROWS[t]], mask[0:ROWS[i], i, :],
                              start=i == 0, stop=i == t)
            done("rank", last)
            ps = take("counts")
            for t in range(3):
                last = mm(ps[0:E, 0:1], mask[0:ROWS[t], t, :], ones[0:ROWS[t], 0:1], start=t == 0, stop=t == 2)
            done("counts", last)
            pe.wait_ge(rounds_ready, 1)
            ps = take("bounds")
            done("bounds", mm(ps[0:E, 0:1], tri_incl[0:E, :], rounds[0:E, :], start=True, stop=True))
            pe.wait_ge(passed_ready, 1)
            ps = take("table")
            mm(ps[0:1, 0:NROUND], ones[0:E, 0:1], passed[0:E, :], start=True, stop=True)
            mm(ps[0:1, NROUND:2 * NROUND], rounds[0:E, :], passed[0:E, :], start=True, stop=True)
            done("table", mm(ps[0:1, 2 * NROUND:2 * NROUND + E], rounds[0:E, :], tri_incl[0:E, :], start=True, stop=True))

            wait_read(pe, FRONT[[n for n in range(len(FRONT)) if n % 8 == B_X][-1]])
            gather(0)
            x_transposes(0)
            pe.wait_ge(softmax_ready, 1)
            ps = take("gate_T")
            for t in range(3):
                r = ROWS[t]
                last = nc.tensor.transpose(ps[0:E, t * P:t * P + r], gate[0:r, t, :], ident[0:r, 0:r])
            done("gate_T", last)

            def combine(n, pieces):
                for i in pieces:
                    b = COMBINE_BANKS[i]
                    if i == 0:
                        pe.wait_ge(O_ready, 2 * n + 2)
                        pe.wait_ge(Pg_ready, n + 1)
                    pe.wait_ge(bank_free[b], front_uses(b) + PER_ROUND[b] * n + COMBINE_BANKS[:i].count(b))
                    if i < 4:
                        t, h = divmod(i, 2)
                        last = mm(bank[b][:, :], P_gate[:, t * P:(t + 1) * P], O_rows[:, h, :], start=True, stop=True)
                    else:
                        for h in range(2):
                            last = mm(bank[b][64 * h:64 * h + 64, :], P_gate[:, 2 * P:NT], O_rows[:, h, :],
                                      start=True, stop=True)
                    last.then_inc(bank_full[b], 1)

            pe.wait_ge(table_ready, 1)
            G = pe.value_load(table[0:1, 159:160], min_val=1, max_val=52)
            pe.wait_ge(b_up_ready, 1)
            with pe.Fori(0, G) as g:
                e = pe.value_load(table[0:1, bass.ds(g, 1)], min_val=0, max_val=E - 1)
                for j in range(2):
                    b = B_UP[j]
                    pe.wait_ge(bank_free[b], g + front_uses(b))
                    if j == 0:
                        pe.wait_ge(sel_ready, g + 1)
                    for h in range(2):
                        at = j * 512 + h * 256
                        mm(bank[b][64 * h:64 * h + 64, :], up_sel,
                           b_up_parts.rearrange("p (g m) -> p g m", g=2)[:, :, at:at + 256], start=True, stop=False)
                    if j == 0:
                        pe.wait_ge(xT_ready, g + 1)
                    for k in range(KC):
                        s = expert_slot(2 * j + k // 4)
                        if k % 4 == 0:
                            pe.wait_ge(chunk_landed[s], e * 32 + 16 * landed_before(s) + 32)
                        w = ring[:, s, :].rearrange("p (g k m) -> p g k m", g=2, k=4)[:, :, k % 4, :]
                        for h in range(2):
                            last = mm(bank[b][64 * h:64 * h + 64, :], x_T[:, k % 4, 64 * (k // 4):64 * (k // 4) + 64],
                                      w[:, :, h * 256:(h + 1) * 256], start=False, stop=k == KC - 1)
                        if k == 3:
                            last.then_inc(chunk_used[s], 1)
                            combine(g, (2 * j, 2 * j + 1))
                    last.then_inc(bank_full[b], 1)
                    if j == 0:
                        gather(g + 1, x_rows_read=g + 1)
                combine(g, (4,))
                pe.wait_ge(gate_ready, g + 1)
                for t in range(3):
                    r = ROWS[t]
                    last = nc.tensor.transpose(bank[B_T][:, t * P:t * P + r], S_gate[0:r, t, :], ident[0:r, 0:r])
                last.then_inc(bank_full[B_T], 1)
                x_transposes(g + 1, xT_read=g + 1)
                pe.wait_ge(act_ready, 2 * g + 2)
                pe.wait_ge(Pg_ready, g + 2)
                for q in range(4):
                    last = nc.tensor.transpose(bank[B_T][:, q * P:(q + 1) * P], act_rows[:, q * P:(q + 1) * P], ident)
                last.then_inc(bank_full[B_T], 1)
                pe.wait_ge(actT_ready, g + 1)
                for k in range(KC):
                    s = expert_slot(4 + k // 4)
                    if k % 4 == 0:
                        pe.wait_ge(chunk_landed[s], e * 16 + 16 * landed_before(s) + 16)
                    q, hh = 2 * (k // 4) + k % 2, (k % 4) // 2
                    for h in range(2):
                        last = mm(bank[B_DOWN][64 * h:64 * h + 64, :], act_T[:, q, 64 * hh:64 * hh + 64],
                                  ring[:, s, (k % 4) * 1024 + h * 512:(k % 4) * 1024 + (h + 1) * 512], start=k == 0, stop=k == KC - 1)
                    if k == 3:
                        last.then_inc(chunk_used[s], 1)
                last.then_inc(bank_full[B_DOWN], 1)
            combine(G, range(5))

        @block.scalar
        def _(act):
            AF = nc.scalar.activation

            def free(name, ins):
                ins.then_inc(bank_free[front_place(name)[0]], 1)

            ps = wait_full(act, "c_T")
            AF(sg_c, ps[:, 0:KC * NC_ROWS].rearrange("p (k b) -> p k b", k=KC), ACT.Sigmoid).then_inc(c_sig_ready, 1)

            def high_of_u(k):
                wait_read(act, f"x_T{k}")
                AF(u_high[:, k, :], u_T[:, k, :], ACT.Copy).then_inc(u_high_ready, 1)

            def split_high(i, between=lambda q: None):
                n = IN_CHUNK + i
                s = front_slot(n)
                if i < 2:
                    wait_chunk_read(act, HIGH_SLOT[i])
                act.wait_ge(chunk_landed[s], 16 * len(in_slot(n)))
                for q in range(4):
                    part = slice(q * 1024, (q + 1) * 1024)
                    AF(ring_parts[:, HIGH_SLOT[i % 2], part], ring[:, s, part], ACT.Copy).then_inc(w_high_ready, 1)
                    between(q)

            wait_full(act, f"x_T{KC - 1}")
            split_high(0, between=lambda q: [high_of_u(k) for k in (2 * q, 2 * q + 1)])
            split_high(1)
            for i, m4 in enumerate(IN_ORDER):
                for m in range(4 * m4, 4 * m4 + 4):
                    ps = wait_full(act, f"proj{m}")
                    if m4 == 0:
                        free(f"proj{m}", AF(b_T[:, m, :], ps[:, 0:NT], ACT.Copy))
                    elif m4 == 1:
                        free(f"proj{m}", AF(c_T[:, m - 4, :], ps[:, 0:NT], ACT.Copy))
                    elif m4 >= 4:
                        dst = ga_T if m < 24 else gb_T
                        free(f"proj{m}", AF(dst[:, (m - 16) % 8, :], ps[:, 0:NT], ACT.Sigmoid))
                if i + 2 < 8:
                    split_high(i + 2)
            for i, (name, r) in enumerate((("state_cp", 2), ("state_cs", 16), ("state_pp", 15), ("state_ps", 120))):
                ps = wait_full(act, name)
                free(name, AF(state_rows[0:r, i, :], ps[0:r, :], ACT.Copy))
            def root(n, row):
                r = row.shape[0]
                if n:
                    act.wait_ge(row_normed, n)
                act.wait_ge(var_ready, n + 1)
                AF(rstd[0:r, :], aggr[0:r, 1:2], ACT.Sqrt).then_inc(sqrt_ready, 1)
                act.wait_ge(rstd_ready, n + 1)
                AF(row, row, ACT.Identity, bias=shift[0:r, :], scale=rstd[0:r, :]).then_inc(row_normed, 1)

            def vT_copy(t):
                r = ROWS[t]
                for half in range(2):
                    ps = wait_full(act, f"v_T{t}{half}")[:, :].rearrange("p (k t) -> p k t", k=4)
                    free(f"v_T{t}{half}", AF(v_T[:, 4 * half:4 * half + 4, t * P:t * P + r], ps[:, :, 0:r], ACT.Copy))

            root(0, hx[:, 0, :])
            ps = wait_full(act, "o2")
            act.wait_ge(row_normed, 1)
            AF(ln_rows[0:NS_TOK, 512:], ps[64:P, :], ACT.Copy).then_inc(o2_moved, 1)
            root(1, hx[0:NS_TOK, 2, :])
            vT_copy(0)
            root(2, hx[:, 1, :])
            vT_copy(2)
            vT_copy(1)
            act.wait_ge(logit_ready, 1)
            AF(gate[:, :, :], eq[:, :, :], ACT.Exp).then_inc(exp_ready, 1)

            def x_copy(n):
                act.wait_ge(bank_full[B_X], front_uses(B_X) + n + 1)
                AF(x_rows[:, :], bank[B_X][:, :], ACT.Copy).then_inc(x_rows_ready, 1)

            def xT_copy(n):
                act.wait_ge(bank_full[B_XT], front_uses(B_XT) + n + 1)
                AF(x_T[:, :, :], bank[B_XT][:, :].rearrange("p (q s) -> p q s", q=4), ACT.Copy).then_inc(xT_ready, 1)

            x_copy(0)
            xT_copy(0)
            act.wait_ge(table_ready, 1)
            G = act.value_load(table[0:1, 159:160], min_val=1, max_val=52)
            with act.Fori(0, G) as g:
                for j in range(2):
                    act.wait_ge(glu_ready, 2 * g + j + 1)
                    AF(sig[:, j, :], glu[:, j, :], ACT.Sigmoid, scale=SWISH).then_inc(sig_ready, 1)
                    if j == 0:
                        x_copy(g + 1)
                act.wait_ge(bank_full[B_T], front_uses(B_T) + 2 * g + 1)
                AF(P_gate[0:SLOTS, :], bank[B_T][0:SLOTS, 0:NT], ACT.Copy).then_inc(Pg_ready, 1)
                xT_copy(g + 1)
                act.wait_ge(bank_full[B_T], front_uses(B_T) + 2 * g + 2)
                AF(act_T[:, :, :], bank[B_T][:, :].rearrange("p (q s) -> p q s", q=4), ACT.Copy).then_inc(actT_ready, 1)
                act.wait_ge(bank_full[B_DOWN], g + front_uses(B_DOWN) + 1)
                for h in range(2):
                    AF(O_rows[0:SLOTS, h, :], bank[B_DOWN][64 * h:64 * h + 64, :], ACT.Copy).then_inc(O_ready, 1)
            AF(rstd, ones[:, 0:1], ACT.Sqrt).then_inc(sqrt_table, 1)
            act.wait_ge(sqrt_table, 1)
            root(3, V[:, 0, :])
            act.wait_ge(bank_full[COMBINE_BANKS[4]], front_uses(6) + 3 * (G + 1))
            AF(y2_rows[0:NS_TOK, :], bank[6][64:P, :], ACT.Copy).then_inc(o2_moved, 1)
            root(4, V[:, 1, :])
            root(5, V[0:NS_TOK, 2, :])

        @block.vector
        def _(dve):
            v = nc.vector
            steps = [0]
            origin = [0]
            step_sem = [dve_step]

            def step(ins):
                steps[0] += 1
                ins.then_inc(step_sem[0], 1)
                dve.wait_ge(step_sem[0], origin[0] + steps[0])

            def signal(ins, sem, value):
                ins.then_inc(sem, 1)
                dve.wait_ge(sem, value)

            def free(name, ins):
                b, n = front_place(name)
                signal(ins, bank_free[b], n + 1)

            TS, TT, STT = v.tensor_scalar, v.tensor_tensor, v.scalar_tensor_tensor
            step(v.memset(mod[:, 0, :], 0.0))
            step(v.memset(z_p[:, :, 0:HIST_C], 0.0))
            step(v.memset(pool_p[:, :, 0:HIST_P], 0.0))
            dve.wait_ge(c_sig_ready, 1)
            ps = wait_full(dve, "c_T")
            free("c_T", TT(sc_T, ps[:, 0:KC * NC_ROWS].rearrange("p (k b) -> p k b", k=KC), sg_c, ALU.mult))
            ps = wait_full(dve, "chan_T")
            free("chan_T", v.tensor_copy(chan, ps[:, 0:16]))
            dve.wait_ge(bada_landed, 64)

            def ada(third):
                ps = wait_full(dve, f"ada{third}")
                for q in range(4):
                    r = slice(32 * q, 32 * q + NC_ROWS)
                    ins = TT(mod[r, third, :], ps[r, :], b_ada_rows[r, third, :], ALU.add)
                    if q < 3:
                        step(ins)
                    else:
                        free(f"ada{third}", ins)

            ada(0)
            ps = wait_full(dve, "mod_T")[:, :].rearrange("p (b r) -> p b r", b=4)
            step(v.tensor_copy(mod_T[:, :, 0:64], ps[:, :, 0:64]))
            free("mod_T", TS(mod_T[:, :, 64:P], ps[:, :, 64:P], 1.0, None, ALU.add))
            for k in range(KC):
                ps = wait_full(dve, f"x_T{k}")
                q, blk = divmod(k, 4)
                sh, sc = mod_T[:, blk, 32 * q:32 * q + NC_ROWS], mod_T[:, blk, 32 * q + 64:32 * q + 64 + NC_ROWS]
                by_seq = lambda t: t.rearrange("p (s t) -> p s t", s=NSEQ)
                wide = lambda t: t[:, 1:NC_ROWS].unsqueeze(2).to_broadcast([P, NSEQ, TSEQ])
                step(TS(u_T[:, k, 0:NP_TOK], ps[:, 0:NP_TOK], sc[:, 0:1], sh[:, 0:1], ALU.mult, ALU.add))
                step(TT(by_seq(u_T[:, k, NP_TOK:]), by_seq(ps[:, NP_TOK:NT]), wide(sc), ALU.mult))
                free(f"x_T{k}", TT(by_seq(u_T[:, k, NP_TOK:]), by_seq(u_T[:, k, NP_TOK:]), wide(sh), ALU.add))
            for k in range(KC):
                dve.wait_ge(u_high_ready, k + 1)
                signal(TT(u_low[:, k, :], u_T[:, k, :], u_high[:, k, :].bitcast(F32), ALU.subtract), u_low_ready, k + 1)
            ps = wait_full(dve, "conv_hist_T")
            free("conv_hist_T", v.tensor_copy(z_s[:, :, :, 0:HIST_C], ps[:, 0:64].rearrange("p (b s t) -> p b s t", b=4, s=NSEQ)))
            ps = wait_full(dve, "pool_hist_T")
            free("pool_hist_T", v.tensor_copy(pool_s[:, :, :, 0:HIST_P], ps[:, 0:480].rearrange("p (b s t) -> p b s t", b=4, s=NSEQ)))
            for b in range(4):
                ps = wait_full(dve, f"proj{8 + b}")
                wait_read(dve, f"proj{4 + b}")
                step(TT(z_p[:, b, HIST_C:], ps[:, 0:NP_TOK], c_T[:, b, 0:NP_TOK], ALU.mult))
                free(f"proj{8 + b}", TT(z_s[:, b, :, HIST_C:], by_seq(ps[:, NP_TOK:NT]), by_seq(c_T[:, b, NP_TOK:]), ALU.mult))
            for b in range(4):
                ps = wait_full(dve, f"proj{12 + b}")
                step(v.tensor_copy(pool_p[:, b, HIST_P:], ps[:, 0:NP_TOK]))
                free(f"proj{12 + b}", v.tensor_copy(pool_s[:, b, :, HIST_P:], by_seq(ps[:, NP_TOK:NT])))
            signal(v.tensor_copy(keep_s, z_s[:, :, :, TSEQ:]), keep_ready, 1)
            signal(v.tensor_copy(keep_ps, pool_s[:, :, :, TSEQ:]), keep_ready, 2)
            for g, w in enumerate(WINDOWS):
                src_p, src_s = pool_p[:, g, :], pool_s[:, g, :, :]
                reach, n = 1, 0
                while reach < w:
                    dp, ds_ = sum_p[:, n % 2, :], sum_s[:, n % 2, :, :]
                    lo = 2 * reach - 1
                    step(TT(dp[:, lo:], src_p[:, lo:], src_p[:, lo - reach:HIST_P + NP_TOK - reach], ALU.add))
                    step(TT(ds_[:, :, lo:], src_s[:, :, lo:], src_s[:, :, lo - reach:HIST_P + TSEQ - reach], ALU.add))
                    src_p, src_s = dp, ds_
                    reach, n = 2 * reach, n + 1
                step(STT(diff_T[:, g, 0:NP_TOK], src_p[:, HIST_P:], 1.0 / w, pool_p[:, g, HIST_P:], ALU.mult, ALU.subtract))
                step(TT(diff_T[:, g, 0:HIST_P], src_p[:, HIST_P:2 * HIST_P], inv_count[:, g, :], ALU.mult))
                step(TT(diff_T[:, g, 0:HIST_P], diff_T[:, g, 0:HIST_P], pool_p[:, g, HIST_P:2 * HIST_P], ALU.subtract))
                signal(STT(by_seq(diff_T[:, g, NP_TOK:]), src_s[:, :, HIST_P:], 1.0 / w, pool_s[:, g, :, HIST_P:],
                           ALU.mult, ALU.subtract), diff_ready, g + 1)
            for b in range(4):
                wait_read(dve, f"proj{b}")
                yp, ys = y_in_T[:, b, 0:NP_TOK], by_seq(y_in_T[:, b, NP_TOK:])
                tap = lambda j: chan[:, 4 * j + b:4 * j + b + 1]
                step(TS(yp, z_p[:, b, 0:NP_TOK], tap(0), None, ALU.mult))
                step(TS(ys, z_s[:, b, :, 0:TSEQ], tap(0), None, ALU.mult))
                for j in (1, 2):
                    step(STT(yp, z_p[:, b, j:j + NP_TOK], tap(j), yp, ALU.mult, ALU.add))
                    step(STT(ys, z_s[:, b, :, j:j + TSEQ], tap(j), ys, ALU.mult, ALU.add))
                signal(TT(y_in_T[:, b, :], y_in_T[:, b, :], b_T[:, b, :], ALU.mult), conv_ready, b + 1)
            for g in range(4):
                ps = wait_full(dve, f"pool{g}")
                free(f"pool{g}", TS(yg_T[:, g, :], ps[:, 0:NT], chan[:, 12 + g:13 + g], None, ALU.mult))
            ada(1)
            for m in range(KC):
                ps = wait_full(dve, f"out_a{m}")
                wait_read(dve, f"proj{16 + m}")
                free(f"out_a{m}", TT(ga_T[:, m, :], ga_T[:, m, :], ps[:, 0:NT], ALU.mult))
            for m in range(KC):
                if m == 4:
                    ada(2)
                ps = wait_full(dve, f"out_b{m}")
                wait_read(dve, f"proj{24 + m}")
                step(TT(gb_T[:, m, :], gb_T[:, m, :], ps[:, 0:NT], ALU.mult))
                free(f"out_b{m}", TT(ga_T[:, m, :], ga_T[:, m, :], gb_T[:, m, :], ALU.add))
            step(v.memset(Y, 0.0))

            normed = [0]

            def normalise(r):
                step(v.bn_aggr(aggr[0:r, :], stats[0:r, :]))
                normed[0] += 1
                signal(TS(aggr[0:r, 1:2], aggr[0:r, 1:2], EPS, None, ALU.add), var_ready, normed[0])
                dve.wait_ge(sqrt_ready, normed[0])
                step(v.reciprocal(rstd[0:r, :], rstd[0:r, :]))
                step(STT(rstd2[0:r, :], rstd[0:r, :], rstd[0:r, :], aggr[0:r, 1:2], ALU.mult, ALU.mult))
                step(TS(rstd2[0:r, :], rstd2[0:r, :], -0.5, 1.5, ALU.mult, ALU.add))
                step(TT(rstd[0:r, :], rstd[0:r, :], rstd2[0:r, :], ALU.mult))
                signal(STT(shift[0:r, :], aggr[0:r, 0:1], -1.0, rstd[0:r, :], ALU.mult, ALU.mult), rstd_ready, normed[0])

            rows_of = lambda t: ring[0:ROWS[t], ROW_SLOT[t // 2], 0:3 * D].rearrange("p (i d) -> p i d", i=3)

            def gain_and_offset(i):
                dve.wait_ge(scale2_landed[i], (16, 16 * NSEQ)[i])
                vec, r = rows_of(2 * i), (P, NS_TOK)[i]
                tmp = ab_rows[0:r, :]
                step(STT(tmp, vec[:, 2, :], 1.0, ring[0:r, ROW_SLOT[1], 3 * D:], ALU.add, ALU.mult))
                step(TT(vec[:, 1, :], vec[:, 1, :], tmp, ALU.add))
                step(STT(vec[:, 2, :], vec[:, 2, :], 1.0, ring[0:r, ROW_SLOT[0], 3 * D:], ALU.add, ALU.mult))

            def residual(t, h):
                r, half = ROWS[t], slice(h * 512, (h + 1) * 512)
                gate1, gated_o = rows_of(t)[:, 0, half], ln_rows[0:r, half]
                if t < 2:
                    ps = wait_full(dve, f"o{t}{h}")
                    free(f"o{t}{h}", TT(gated_o, ps[0:r, :], gate1, ALU.mult))
                elif h == 0:
                    ps = wait_full(dve, "o2")
                    free("o2", TT(gated_o, ps[0:r, :], gate1, ALU.mult))
                else:
                    dve.wait_ge(o2_moved, 1)
                    step(TT(gated_o, gated_o, gate1, ALU.mult))
                step(STT(hx[0:r, t, half], hx[0:r, t, half], ALPHA, gated_o, ALU.mult, ALU.add))
                step(v.bn_stats(stats[0:r, 6 * h:6 * h + 6], hx[0:r, t, half]))

            def v_rows(t):
                i, r, vec = TILE_ORDER.index(t), ROWS[t], rows_of(t)
                dve.wait_ge(row_normed, i + 1)
                step(TT(V[0:r, t, :], hx[0:r, t, :], vec[:, 2, :], ALU.mult))
                signal(TT(V[0:r, t, :], V[0:r, t, :], vec[:, 1, :], ALU.add), v_ready, i + 1)

            dve.wait_ge(norm1_landed, 16 * (3 + NSEQ))
            dve.wait_ge(x_landed, 64)
            dve.wait_ge(out_stored, 64)
            residual(0, 0)
            gain_and_offset(0)
            residual(0, 1)
            normalise(P)
            gain_and_offset(1)
            residual(2, 0)
            residual(2, 1)
            v_rows(0)
            normalise(NS_TOK)
            residual(1, 0)
            v_rows(2)
            residual(1, 1)
            normalise(P)
            v_rows(1)

            dve.wait_ge(router_landed, 32)
            step(v.memset(L, 0.0))
            step(v.memset(top, 0.0))
            step(v.memset(top_f, 0.0))
            for t in TILE_ORDER:
                r = ROWS[t]
                ps = wait_full(dve, f"logits{t}")
                free(f"logits{t}", TT(L[0:r, t, :], ps[0:r, 0:E], b_router[0:r, :], ALU.add))
                step(v.max(top[0:r, t, :], L[0:r, t, :]))
                step(v.max_index(top_index[0:r, t, :], top[0:r, t, :], L[0:r, t, :]))
                step(v.tensor_copy(top_f[0:r, t, :], top_index[0:r, t, :]))
            by_e = lambda t: t.to_broadcast([P, 3, E])
            experts = iota[:, 0:E].unsqueeze(1).to_broadcast([P, 3, E])
            signal(TT(eq, L, by_e(top[:, :, 0:1]), ALU.subtract), logit_ready, 1)
            step(TT(mask, experts, by_e(top_f[:, :, 0:1]), ALU.is_equal))
            dve.wait_ge(exp_ready, 1)
            for k in range(1, TOPK):
                step(TT(eq, experts, by_e(top_f[:, :, k:k + 1]), ALU.is_equal))
                ins = TT(mask, mask, eq, ALU.add)
                step(ins) if k < TOPK - 1 else signal(ins, mask_ready, 1)
            step(TT(gate, gate, mask, ALU.mult))
            step(v.reduce_sum(gsum, gate, AX_X))
            step(v.reciprocal(gsum, gsum))
            signal(TT(gate, gate, by_e(gsum.unsqueeze(2)), ALU.mult), softmax_ready, 1)
            by_slot = lambda t: t.to_broadcast([P, 3, SLOTS])

            def one_hots(n, e, base):
                slots = iota[:, bass.ds(base, SLOTS)].unsqueeze(1).to_broadcast([P, 3, SLOTS])
                signal(TT(S, slots, by_slot(rank[:, :, bass.ds(e, 1)]), ALU.is_equal), S_ready, n + 1)

            def select_bias(n, e):
                signal(v.tensor_copy(up_sel, sel3[:, bass.ds(e, 1)].to_broadcast([P, SLOTS])), sel_ready, n + 1)

            def gated(n, e):
                signal(TT(S_gate[:, :, 0:SLOTS], S, by_slot(gate[:, :, bass.ds(e, 1)]), ALU.mult), gate_ready, n + 1)

            ps = wait_full(dve, "counts")
            free("counts", v.tensor_copy(count[0:E, :], ps[0:E, 0:1]))
            step(TS(rounds[0:E, :], count[0:E, :], float(SLOTS), 1.0, ALU.is_gt, ALU.add))
            for i in range(2, MAXR):
                ins = STT(rounds[0:E, :], count[0:E, :], float(i * SLOTS), rounds[0:E, :], ALU.is_gt, ALU.add)
                step(ins) if i < MAXR - 1 else signal(ins, rounds_ready, 1)
            ps = wait_full(dve, "rank")
            step(v.memset(rank, -1.0))
            for t in range(3):
                r = ROWS[t]
                ins = STT(rank[0:r, t, :], ps[0:r, t * E:(t + 1) * E], 1.0, mask[0:r, t, :], ALU.add, ALU.mult)
                step(ins) if t < 2 else free("rank", ins)
            for t in range(3):
                step(TS(rank[0:ROWS[t], t, :], rank[0:ROWS[t], t, :], -1.0, None, ALU.add))
            ps = wait_full(dve, "bounds")
            free("bounds", v.tensor_copy(bound[0:E, :], ps[0:E, 0:1]))
            signal(TS(passed[0:E, :], iota[0:E, 0:NROUND], bound[0:E, :], None, ALU.is_ge), passed_ready, 1)
            one_hots(0, 0, 0)
            ps = wait_full(dve, "table")
            step(TS(table[0:1, 0:NROUND], ps[0:1, 0:NROUND], float(E - 1), None, ALU.min))
            step(TT(base_f[0:1, :], iota[0:1, 0:NROUND], ps[0:1, NROUND:2 * NROUND], ALU.subtract))
            step(TS(table[0:1, NROUND:2 * NROUND], base_f[0:1, :], float(SLOTS), None, ALU.mult))
            free("table", v.tensor_copy(table[0:1, 2 * NROUND:2 * NROUND + E], ps[0:1, 2 * NROUND:2 * NROUND + E]))
            step(v.memset(S_gate, 0.0))
            step(v.memset(P_gate, 0.0))
            signal(v.memset(stats[0:1, 0:1], 0.0), table_ready, 1)
            ps = wait_full(dve, "gate_T")
            free("gate_T", v.tensor_copy(P_gate[0:E, :], ps[0:E, 0:NT]))
            dve.wait_ge(b_down_landed, 16)
            signal(v.memset(stats[0:1, 0:1], 0.0), Pg_ready, 1)
            signal(v.memset(stats[0:1, 0:1], 0.0), O_ready, 1)
            signal(v.memset(stats[0:1, 0:1], 0.0), O_ready, 2)

            G = dve.value_load(table[0:1, 159:160], min_val=1, max_val=52)

            def add_up(n, pieces):
                for i in pieces:
                    b = COMBINE_BANKS[i]
                    value = front_uses(b) + PER_ROUND[b] * n + COMBINE_BANKS[:i + 1].count(b)
                    dve.wait_ge(bank_full[b], value)
                    signal(TT(Y[:, i, :], Y[:, i, :], bank[b][:, :], ALU.add), bank_free[b], value)

            select_bias(0, 0)
            gated(0, 0)
            before = steps[0]
            PER_LOOP = 2
            with dve.Fori(0, G) as g:
                steps[0] = 0
                origin[0] = g * PER_LOOP + before
                e = dve.value_load(table[0:1, bass.ds(g + 1, 1)], min_val=0, max_val=E - 1)
                base = dve.value_load(table[0:1, bass.ds(g + NROUND + 1, 1)], min_val=0, max_val=(MAXR - 1) * SLOTS)
                dve.wait_ge(bank_full[B_X], g + front_uses(B_X) + 1)
                one_hots(g + 1, e, base)
                for j in range(2):
                    add_up(g, (2 * j, 2 * j + 1))
                    b = B_UP[j]
                    dve.wait_ge(bank_full[b], g + front_uses(b) + 1)
                    signal(TS(glu[:, j, :], bank[b][:, 0:256], LIMIT, None, ALU.min), glu_ready, 2 * g + j + 1)
                    signal(TS(lin[:, j, :], bank[b][:, 256:512], -LIMIT, LIMIT, ALU.max, ALU.min), bank_free[b],
                           g + front_uses(b) + 1)
                    step(STT(lin[:, j, :], lin[:, j, :], 1.0, glu[:, j, :], ALU.add, ALU.mult))
                    dve.wait_ge(sig_ready, 2 * g + j + 1)
                    signal(TT(act_rows[:, j * 256:(j + 1) * 256], lin[:, j, :], sig[:, j, :], ALU.mult), act_ready, 2 * g + j + 1)
                select_bias(g + 1, e)
                add_up(g, (4,))
                dve.wait_ge(bank_full[B_T], g * 2 + front_uses(B_T) + 1)
                gated(g + 1, e)
                assert steps[0] == PER_LOOP
            steps[0], origin[0], step_sem[0] = 0, 0, tail_step
            dve.wait_ge(tail_landed, 16 * (3 + NSEQ))
            dve.wait_ge(h_ready, 3)
            dve.wait_ge(bank_full[B_X], G + front_uses(B_X) + 1)
            step(v.tensor_copy(Y_2[0:NS_TOK, :], Y[64:P, 4, :]))
            gate2 = lambda t, h: tail_rows[0:ROWS[t], (0 if t < 2 else D) + h * 512:(0 if t < 2 else D) + (h + 1) * 512]
            for t in range(3):
                r = ROWS[t]
                for h in range(2):
                    f = Y[0:r, 2 * t + h, :] if t < 2 else (Y[0:r, 4, :], Y_2[0:r, :])[h]
                    step(TT(V[0:r, t, h * 512:(h + 1) * 512], f, gate2(t, h), ALU.mult))
                step(TT(V[0:r, t, :], V[0:r, t, :], hx[0:r, t, :], ALU.add))
            used = {6: 0, 7: 0}
            for t in range(3):
                r = ROWS[t]
                for h in range(2):
                    i = 2 * t + h
                    if i < 5:
                        b = COMBINE_BANKS[i]
                        used[b] += 1
                        value = G * PER_ROUND[b] + (front_uses(b) + used[b])
                        dve.wait_ge(bank_full[b], value)
                        if i == 4:
                            dve.wait_ge(o2_moved, 2)
                        signal(TT(Y[0:r, i, :], bank[b][0:r, :], gate2(t, h), ALU.mult), bank_free[b], value)
                        share = Y[0:r, i, :]
                    else:
                        step(TT(y2_rows[0:r, :], y2_rows[0:r, :], gate2(t, h), ALU.mult))
                        share = y2_rows[0:r, :]
                    half = V[0:r, t, h * 512:(h + 1) * 512]
                    step(TT(half, half, share, ALU.add))
                    step(v.bn_stats(stats[0:r, 6 * h:6 * h + 6], half))
                normalise(r)
            r = ROWS[2]
            dve.wait_ge(row_normed, 6)
            step(TT(V[0:r, 2, :], V[0:r, 2, :], tail_rows[0:r, 2 * D:3 * D], ALU.mult))
            signal(TT(V[0:r, 2, :], V[0:r, 2, :], tail_rows[0:r, 3 * D:], ALU.add), y_ready, 1)


INPUTS = ["x_prompt", "x_sample", "c_prompt", "c_sample", "state_conv", "state_pool", "w_ada", "b_ada", "w_in",
          "conv_w", "w_out_a", "w_pool", "ls_pool", "w_out_b", "w_o", "ln1_g", "ln1_b", "w_router", "b_router",
          "w_up", "b_up", "w_down", "b_down", "ln2_g", "ln2_b"]
OUTPUTS = {"y_p": (1, NP_TOK, D), "y_s": (NSEQ, TSEQ, D), "conv_p": (1, 1, HIST_C, DC), "pool_p": (1, 1, HIST_P, DC),
           "conv_s": (1, NSEQ, HIST_C, DC), "pool_s": (1, NSEQ, HIST_P, DC)}


def constants():
    c = np.zeros((P, C_N), np.float32)
    c[:, C_ID:C_ID + P] = np.eye(P)
    c[:, C_TRI:C_TRI + P] = np.triu(np.ones((P, P)), 1)
    c[:, C_ONE:C_ONE + P] = 1.0
    c[:, C_TRI1:C_TRI1 + E] = np.triu(np.ones((P, E)))
    c[:, C_IOTA:C_IOTA + NT] = np.arange(NT)
    for g, w in enumerate(WINDOWS):
        c[:, C_INV + g * HIST_P:C_INV + (g + 1) * HIST_P] = 1.0 / np.minimum(w, np.arange(HIST_P) + 1)
    for q in range(3):
        c[32 * q:32 * q + E, C_SEL:C_SEL + E] = np.eye(E)
    return c


def kernel(**inputs):
    import concourse.bacc as bacc
    from concourse.bass_utils import run_bass_kernel_spmd

    nc = bacc.Bacc("TRN2", target_bir_lowering=False, num_devices=1)
    arrays = {f"in_{n}": np.ascontiguousarray(inputs[n]) for n in INPUTS}
    arrays["in_const"] = constants()
    a = {n: nc.dram_tensor(f"in_{n}", arrays[f"in_{n}"].shape, F32, kind="ExternalInput").ap() for n in INPUTS + ["const"]}
    o = {n: nc.dram_tensor(f"out_{n}", shape, F32, kind="ExternalOutput").ap() for n, shape in OUTPUTS.items()}
    program(nc, a, o)
    r = run_bass_kernel_spmd(nc, [arrays], core_ids=[0]).results[0]
    return tuple(r[f"out_{n}"] for n in OUTPUTS)
```
